# Optimizing a Trainium2 kernel written in Bass

```python
import math
import jax, jax.numpy as jnp
from jax import lax
import numpy as np

D_MODEL = 1024
BATCH = 1
SEQ = 512
DEPTH = 1

HEAD_DIM = 64
N_HEADS_MOBA = 8
N_HEADS_SWA = 8
N_KV_SWA = 2
N_HEADS = N_HEADS_MOBA + N_HEADS_SWA
MIX_WIDTH = N_HEADS * HEAD_DIM
W_MOBA = N_HEADS_MOBA * HEAD_DIM
W_SWA = N_HEADS_SWA * HEAD_DIM
W_SWA_KV = N_KV_SWA * HEAD_DIM
IN_COLS = 3 * W_MOBA + W_SWA + 2 * W_SWA_KV
IN_SPLITS = [W_MOBA, 2 * W_MOBA, 3 * W_MOBA, 3 * W_MOBA + W_SWA, 3 * W_MOBA + W_SWA + W_SWA_KV]
MOBA_BLOCK = 256
MOBA_TOPK = 3
MOBA_Q_CHUNK = 64
SWA_WINDOW = 128
SWA_BLOCK = 128
NUM_BUCKETS = 32
MAX_DISTANCE = 128
D_FF = 2816
RMS_EPS = 1e-6
FFN_RES_WEIGHT = 0.5
NEG = -1e30

kernel_name = "hymba_moba_swa_macaron_layer"

def rms_norm(x, g):
    xf = x.astype(jnp.float32)
    y = xf * lax.rsqrt(jnp.mean(xf * xf, axis=-1, keepdims=True) + RMS_EPS)
    return (y * g.astype(jnp.float32)).astype(x.dtype)

def swiglu(x, w_gate, w_up, w_down):
    return (jax.nn.silu(x @ w_gate) * (x @ w_up)) @ w_down

def t5_bucket(dist):
    n = jnp.maximum(dist, 0)
    max_exact = NUM_BUCKETS // 2
    nf = jnp.maximum(n, 1).astype(jnp.float32)
    large = max_exact + (jnp.log(nf / max_exact) / math.log(MAX_DISTANCE / max_exact)
                         * (NUM_BUCKETS - max_exact)).astype(jnp.int32)
    large = jnp.minimum(large, NUM_BUCKETS - 1)
    return jnp.where(n < max_exact, n, large)

def moba_attention(q, k, v, bias_tab):
    B, T, H, hd = q.shape
    nb = -(-T // MOBA_BLOCK)
    tp = nb * MOBA_BLOCK
    padw = ((0, 0), (0, tp - T), (0, 0), (0, 0))
    q, k, v = [jnp.pad(a, padw).transpose(0, 2, 1, 3) for a in (q, k, v)]
    kb = k.reshape(B, H, nb, MOBA_BLOCK, hd)
    vb = v.reshape(B, H, nb, MOBA_BLOCK, hd)
    scale = hd ** -0.5
    k_mean = jnp.mean(kb.astype(jnp.float32), axis=3)
    gate = jnp.einsum('bhtd,bhnd->bhtn', q.astype(jnp.float32), k_mean)
    q_blk = jnp.arange(tp) // MOBA_BLOCK
    past = jnp.arange(nb)[None, :] < q_blk[:, None]
    gate = jnp.where(past, gate, NEG)
    k_sel = min(MOBA_TOPK, nb)
    _, sel = lax.top_k(gate, k_sel)
    sel_valid = sel < q_blk[:, None]
    offs = jnp.arange(MOBA_BLOCK)
    h_idx = jnp.arange(H)[:, None, None, None]
    gather_blocks = jax.vmap(jax.vmap(lambda blocks, idx: blocks[idx]))

    def chunk(c):
        start = c * MOBA_Q_CHUNK
        qc = lax.dynamic_slice_in_dim(q, start, MOBA_Q_CHUNK, axis=2)
        sc = lax.dynamic_slice_in_dim(sel, start, MOBA_Q_CHUNK, axis=2)
        vc = lax.dynamic_slice_in_dim(sel_valid, start, MOBA_Q_CHUNK, axis=2)
        qpos = start + jnp.arange(MOBA_Q_CHUNK)
        k_g = gather_blocks(kb, sc)
        v_g = gather_blocks(vb, sc)
        s_sel = jnp.einsum('bhcd,bhcjsd->bhcjs', qc, k_g).astype(jnp.float32) * scale
        kpos = sc[..., None] * MOBA_BLOCK + offs
        bias_sel = bias_tab[h_idx, t5_bucket(qpos[:, None, None] - kpos)].astype(jnp.float32)
        s_sel = jnp.where(vc[..., None], s_sel + bias_sel, NEG)
        blk = start // MOBA_BLOCK
        k_own = lax.dynamic_index_in_dim(kb, blk, axis=2, keepdims=False)
        v_own = lax.dynamic_index_in_dim(vb, blk, axis=2, keepdims=False)
        s_own = jnp.einsum('bhcd,bhsd->bhcs', qc, k_own).astype(jnp.float32) * scale
        dist_own = qpos[:, None] - (blk * MOBA_BLOCK + offs)[None, :]
        bias_own = bias_tab[:, t5_bucket(dist_own)].astype(jnp.float32)
        s_own = jnp.where(dist_own >= 0, s_own + bias_own, NEG)
        logits = jnp.concatenate([s_sel.reshape(B, H, MOBA_Q_CHUNK, k_sel * MOBA_BLOCK), s_own], axis=-1)
        p = jax.nn.softmax(logits, axis=-1).astype(v.dtype)
        p_sel = p[..., :k_sel * MOBA_BLOCK].reshape(B, H, MOBA_Q_CHUNK, k_sel, MOBA_BLOCK)
        p_own = p[..., k_sel * MOBA_BLOCK:]
        return (jnp.einsum('bhcjs,bhcjsd->bhcd', p_sel, v_g)
                + jnp.einsum('bhcs,bhsd->bhcd', p_own, v_own))

    outs = lax.map(chunk, jnp.arange(tp // MOBA_Q_CHUNK))
    out = outs.transpose(1, 2, 0, 3, 4).reshape(B, H, tp, hd)[:, :, :T]
    return out.transpose(0, 2, 1, 3)

def swa_attention(q, k, v, sinks, bias_tab):
    B, T, Hq, hd = q.shape
    Hkv = k.shape[2]
    G = Hq // Hkv
    nb = T // SWA_BLOCK
    qb = q.reshape(B, nb, SWA_BLOCK, Hkv, G, hd)
    kb = k.reshape(B, nb, SWA_BLOCK, Hkv, hd)
    vb = v.reshape(B, nb, SWA_BLOCK, Hkv, hd)
    shift = ((0, 0), (1, 0), (0, 0), (0, 0), (0, 0))
    kw = jnp.concatenate([jnp.pad(kb, shift)[:, :-1], kb], axis=2)
    vw = jnp.concatenate([jnp.pad(vb, shift)[:, :-1], vb], axis=2)
    logits = jnp.einsum('bnqkgd,bnskd->bkgnqs', qb, kw).astype(jnp.float32) * (hd ** -0.5)
    qi = jnp.arange(SWA_BLOCK)
    ki = jnp.arange(2 * SWA_BLOCK) - SWA_BLOCK
    dist = qi[:, None] - ki[None, :]
    in_win = (dist >= 0) & (dist < SWA_WINDOW)
    kpos = jnp.arange(nb)[:, None] * SWA_BLOCK + ki[None, :]
    valid = in_win[None] & (kpos[:, None, :] >= 0)
    bias = bias_tab[:, t5_bucket(dist)].astype(jnp.float32).reshape(Hkv, G, 1, SWA_BLOCK, 2 * SWA_BLOCK)
    logits = jnp.where(valid, logits + bias, NEG)
    sink = jnp.broadcast_to(sinks.astype(jnp.float32).reshape(Hkv, G, 1, 1, 1),
                            (B, Hkv, G, nb, SWA_BLOCK, 1))
    p = jax.nn.softmax(jnp.concatenate([logits, sink], axis=-1), axis=-1)[..., :-1]
    out = jnp.einsum('bkgnqs,bnskd->bnqkgd', p.astype(v.dtype), vw)
    return out.reshape(B, T, Hq, hd)

def hybrid_mixer(h, w_in, rel_bias, moba_out_g, swa_sinks, swa_out_g, w_out):
    B, T, _ = h.shape
    proj = h @ w_in
    qa, ka, va, qs, ks, vs = jnp.split(proj, IN_SPLITS, axis=-1)
    bias_tab = rel_bias.T
    oa = moba_attention(qa.reshape(B, T, N_HEADS_MOBA, HEAD_DIM),
                        ka.reshape(B, T, N_HEADS_MOBA, HEAD_DIM),
                        va.reshape(B, T, N_HEADS_MOBA, HEAD_DIM),
                        bias_tab[:N_HEADS_MOBA])
    ob = swa_attention(qs.reshape(B, T, N_HEADS_SWA, HEAD_DIM),
                       ks.reshape(B, T, N_KV_SWA, HEAD_DIM),
                       vs.reshape(B, T, N_KV_SWA, HEAD_DIM),
                       swa_sinks, bias_tab[N_HEADS_MOBA:])
    oa = rms_norm(oa.reshape(B, T, W_MOBA), moba_out_g)
    ob = rms_norm(ob.reshape(B, T, W_SWA), swa_out_g)
    return jnp.concatenate([oa, ob], axis=-1) @ w_out

def setup_inputs(seed: int = 0) -> dict:
    key = jax.random.key(seed)
    ks = jax.random.split(key, 19)
    f32 = jnp.float32

    def gain(k, n):
        return 1.0 + 0.05 * jax.random.normal(k, (DEPTH, n), f32)

    def dense(k, fan_in, fan_out):
        return jax.random.normal(k, (DEPTH, fan_in, fan_out), f32) * fan_in ** -0.5

    return {
        "x": jax.random.normal(ks[0], (BATCH, SEQ, D_MODEL), f32),
        "ffn1_pre_g": gain(ks[1], D_MODEL),
        "ffn1_w_gate": dense(ks[2], D_MODEL, D_FF),
        "ffn1_w_up": dense(ks[3], D_MODEL, D_FF),
        "ffn1_w_down": dense(ks[4], D_FF, D_MODEL),
        "ffn1_post_g": gain(ks[5], D_MODEL),
        "mix_pre_g": gain(ks[6], D_MODEL),
        "w_in": dense(ks[7], D_MODEL, IN_COLS),
        "rel_bias": 0.5 * jax.random.normal(ks[8], (NUM_BUCKETS, N_HEADS), f32),
        "moba_out_g": gain(ks[9], W_MOBA),
        "swa_sinks": 0.5 * jax.random.normal(ks[10], (DEPTH, N_HEADS_SWA), f32),
        "swa_out_g": gain(ks[11], W_SWA),
        "w_out": dense(ks[12], MIX_WIDTH, D_MODEL),
        "mix_post_g": gain(ks[13], D_MODEL),
        "ffn2_pre_g": gain(ks[14], D_MODEL),
        "ffn2_w_gate": dense(ks[15], D_MODEL, D_FF),
        "ffn2_w_up": dense(ks[16], D_MODEL, D_FF),
        "ffn2_w_down": dense(ks[17], D_FF, D_MODEL),
        "ffn2_post_g": gain(ks[18], D_MODEL),
    }

def reference(x, ffn1_pre_g, ffn1_w_gate, ffn1_w_up, ffn1_w_down, ffn1_post_g,
              mix_pre_g, w_in, rel_bias, moba_out_g, swa_sinks, swa_out_g, w_out, mix_post_g,
              ffn2_pre_g, ffn2_w_gate, ffn2_w_up, ffn2_w_down, ffn2_post_g):
    for l in range(DEPTH):
        h = swiglu(rms_norm(x, ffn1_pre_g[l]), ffn1_w_gate[l], ffn1_w_up[l], ffn1_w_down[l])
        x = x + FFN_RES_WEIGHT * rms_norm(h, ffn1_post_g[l])
        h = hybrid_mixer(rms_norm(x, mix_pre_g[l]), w_in[l], rel_bias, moba_out_g[l],
                         swa_sinks[l], swa_out_g[l], w_out[l])
        x = x + rms_norm(h, mix_post_g[l])
        h = swiglu(rms_norm(x, ffn2_pre_g[l]), ffn2_w_gate[l], ffn2_w_up[l], ffn2_w_down[l])
        x = x + FFN_RES_WEIGHT * rms_norm(h, ffn2_post_g[l])
    return x


_drawn_inputs = setup_inputs


def setup_inputs(seed=0):
    import zlib

    import numpy as np

    out = dict(_drawn_inputs(seed))
    spreads = {}
    factors = {'swa_sinks': 8.0, 'ffn2_post_g': 3.67}
    for name, (base, spread) in spreads.items():
        noise = np.random.default_rng([zlib.crc32(name.encode()), seed]).standard_normal(out[name].shape)
        drawn = base * np.exp(spread * noise) if base else spread * noise
        out[name] = __import__('jax').numpy.asarray(drawn.astype(out[name].dtype))
    for name, factor in factors.items():
        out[name] = (out[name] * factor).astype(out[name].dtype)
    return out
```

```python
import math
from contextlib import ExitStack

import numpy as np
import concourse.bass as bass
from concourse import mybir

ALU = mybir.AluOpType
ACT = mybir.ActivationFunctionType
F32 = mybir.dt.float32
F32R = mybir.dt.float32r
BF16 = mybir.dt.bfloat16

P = 128
D = 1024
T = 512
F = 2816
KD = D // P
NT = T // P
NF = F // P
HD = 64
W_MOBA = 512
W_SWA = 512
BUCKETS = 32
MAX_DISTANCE = 128
WINDOW = 128
EPS = 1e-6
NEG = -1e30
BIG = 3.0e38
SCALE = HD ** -0.5

RING = 4
UP1 = 0
DOWN1 = UP1 + 2 * NF
IN = DOWN1 + NF
OUT = IN + 18
UP2 = OUT + D // P
DOWN2 = UP2 + 2 * NF
PANELS = DOWN2 + NF
LEAD = 2

PAIRS = 4
UNITS = 16
STEPS = UNITS + 3
TAB = 640


def bucket_ranges():
    exact = BUCKETS // 2

    def bucket(n):
        if n < exact:
            return n
        large = exact + int(np.float32(np.log(np.float32(n) / np.float32(exact)) / np.float32(math.log(MAX_DISTANCE / exact)))
                            * np.float32(BUCKETS - exact))
        return min(large, BUCKETS - 1)

    of = [bucket(n) for n in range(T)]
    return [(of.index(b), T - of[::-1].index(b)) for b in range(BUCKETS)]


def build(nc, x, ffn1_pre_g, ffn1_w_gate, ffn1_w_up, ffn1_w_down, ffn1_post_g, mix_pre_g, w_in, rel_bias,
          moba_out_g, swa_sinks, swa_out_g, w_out, mix_post_g, ffn2_pre_g, ffn2_w_gate, ffn2_w_up,
          ffn2_w_down, ffn2_post_g, out):
    ctx = ExitStack()
    with ctx:
        def sb(name, shape, dt=F32, scope=ctx):
            return scope.enter_context(nc.sbuf_tensor(name, shape, dt))

        def sem(name):
            return ctx.enter_context(nc.semaphore(name))

        ps = ctx.enter_context(nc.psum_tensor("ps", [P, 8, 512], F32))
        xres = sb("xres", [P, NT, D])
        xT_hi = sb("xT_hi", [P, KD, T], F32R)
        xT_lo = sb("xT_lo", [P, KD, T], F32R)
        raw = sb("raw", [P, RING, 1024])
        w_hi = sb("w_hi", [P, RING, 1024], F32R)
        w_lo = sb("w_lo", [P, RING, 1024], F32R)
        g_a = sb("g_a", [P, D])
        g_b = sb("g_b", [P, D])
        g_c = sb("g_c", [P, D])
        g_d = sb("g_d", [P, D])
        xn = sb("xn", [P, 2, D])
        tmp = sb("tmp", [P, D])
        junk = sb("junk", [P, 2, D], BF16)
        ident = sb("ident", [P, P])
        expo = sb("expo", [P, 2])
        ssy = sb("ssy", [P, 12])
        msy = sb("msy", [P, 12])
        rsy = sb("rsy", [P, 12])
        ssx = sb("ssx", [P, 16, 2])
        msx = sb("msx", [P, 16, 2])
        rsx = sb("rsx", [P, 16, 2])
        sinks = sb("sinks", [P, 8])
        nsink = sb("nsink", [P, 8])
        relT = sb("relT", [8, 2, BUCKETS])
        rows = sb("rows", [8, 2, TAB])
        with ExitStack() as only_ffn:
            hT = sb("hT", [P, NF, T], F32, only_ffn)
            hs_hi = sb("hs_hi", [P, RING, T], F32R, only_ffn)
            hs_lo = sb("hs_lo", [P, RING, T], F32R, only_ffn)
        ksT = sb("ksT", [P, T])
        vs = sb("vs", [P, NT, P])
        vT = sb("vT", [P, T])
        qs_next, qm_next, km_next = sb("qs_next", [P, T]), sb("qm_next", [P, T]), sb("km_next", [P, T])
        vm_next = sb("vm_next", [P, NT, P])
        qs, qm, km = sb("qs", [P, T]), sb("qm", [P, T]), sb("km", [P, T])
        vm = sb("vm", [P, NT, P])
        bias_s = sb("bias_s", [P, 2, 2 * P])
        bias_m = sb("bias_m", [P, 2, T])
        nsink_now = sb("nsink_now", [P, 2])
        s_win = sb("s_win", [P, 2, 2, 2 * P + 1])
        s_moba = sb("s_moba", [P, 2, T])
        prob = sb("prob", [P, RING, T + 2])
        pT = sb("pT", [P, 2, T])
        nmax = sb("nmax", [P, UNITS])
        psumrow = sb("psumrow", [P, UNITS])
        rinv = sb("rinv", [P, UNITS])
        att = sb("att", [P, NT, D])

        PITCH = 24 * TAB
        scratch = nc.dram_tensor("bias_rows", (P * PITCH,), F32, kind="Internal").ap()
        skewed = scratch[P - 1:P - 1 + P * (PITCH - 1)].rearrange("(q r) -> q r", r=PITCH - 1)

        x_loaded = [sem(f"x_loaded{t}") for t in range(NT)]
        gain_a, gain_b, gain_c, gain_d = sem("gain_a"), sem("gain_b"), sem("gain_c"), sem("gain_d")
        small_loaded = sem("small_loaded")
        raw_loaded = [sem(f"raw_loaded{s}") for s in range(RING)]
        hi_ready, lo_ready, panel_used = sem("hi_ready"), sem("lo_ready"), sem("panel_used")
        silu_done, h_done = sem("silu_done"), sem("h_done")
        hs_hi_ready, hs_lo_ready = sem("hs_hi_ready"), sem("hs_lo_ready")
        y_done, ssy_done, rsy_done = sem("y_done"), sem("ssy_done"), sem("rsy_done")
        branch_done, x_ready = sem("branch_done"), sem("x_ready")
        ssx_done, rsx_done, xn_ready = sem("ssx_done"), sem("rsx_done"), sem("xn_ready")
        xT_in_psum, xT_hi_ready, xT_lo_ready = sem("xT_in_psum"), sem("xT_hi_ready"), sem("xT_lo_ready")
        const_ready, pool_step, ident_ready = sem("const_ready"), sem("pool_step"), sem("ident_ready")
        ms_done = sem("ms_done")
        rows_ready, rows_stored = sem("rows_ready"), sem("rows_stored")
        nsink_ready = sem("nsink_ready")
        turned_values, evac_a, evac_d = sem("turned_values"), sem("evac_a"), sem("evac_d")
        qs_ready, qk_ready, vm_ready = sem("qs_ready"), sem("qk_ready"), sem("vm_ready")
        bias_s_loaded, bias_m_loaded, sink_ready = sem("bias_s_loaded"), sem("bias_m_loaded"), sem("sink_ready")
        scores_done, logits_done, exp_done = sem("scores_done"), sem("logits_done"), sem("exp_done")
        pT_in_psum, pT_by_act, pT_by_dve = sem("pT_in_psum"), sem("pT_by_act"), sem("pT_by_dve")
        pv_done, rinv_done, att_done = sem("pv_done"), sem("rinv_done"), sem("att_done")
        out_stored = sem("out_stored")
        dve_held, pool_held = sem("dve_held"), sem("pool_held")

        def bank2(tok):
            return ps[:, 2 * tok:2 * tok + 2, :].rearrange("p b n -> p (b n)")

        def sums_of(n):
            return n + 1 + min(max(n - 7, 0), NT)

        def unit(k):
            win, e, qt = k < 8, k // 4 % 2, k % 4
            return win, e, qt, list(range(max(qt - 1, 0), qt + 1)) if win else list(range(qt + 1))

        def wait_loaded(eng, c, i=0):
            n = c // RING + i + 1
            if c % RING == 0 and c >= IN:
                n = n + (c // RING + i - IN // RING if c < UP2 else UP2 // RING - 1 - IN // RING)
            eng.wait_ge(raw_loaded[c % RING], 16 * n)

        def wait_split(eng, c, i=0):
            eng.wait_ge(hi_ready, c + 4 * i + 1)
            eng.wait_ge(lo_ready, c + 4 * i + 1)

        def stationary_weights(c):
            return [w[:, c % RING, :].rearrange("p (k f) -> p k f", f=P) for w in (w_hi, w_lo)]

        block = ctx.enter_context(nc.Block())

        def hold_here(eng, counter):
            eng.sem_inc(counter, 1)

        @block.sync
        def _(sp):
            for t in range(NT):
                sp.dma_start(xres[:, t, :], x[0, t * P:(t + 1) * P, :]).then_inc(x_loaded[t], 16)

            def wait_free(c, i):
                sp.wait_ge(lo_ready, c + 4 * i - RING + 1)

            def column_panel(c, i, w, col, free=True):
                if free:
                    wait_free(c, i)
                sp.dma_start(raw[:, c % RING, :].rearrange("p (k f) -> p k f", f=P),
                             w[0, :, bass.ds(col, P)].rearrange("(k p) f -> p k f", p=P)) \
                    .then_inc(raw_loaded[c % RING], 16)

            def row_panel(c, i, w, row):
                wait_free(c, i)
                parts = 2 if c % RING == 0 and IN <= c < UP2 else 1
                for n in range(parts):
                    cols = slice(n * (D // parts), (n + 1) * (D // parts))
                    sp.dma_start(raw[:, c % RING, cols], w[0, bass.ds(row, P), cols]).then_inc(raw_loaded[c % RING], 16)

            def up_panels(base, w_gate, w_up):
                if base == 0:
                    for j in range(RING):
                        column_panel(j, 0, (w_gate, w_up)[j % 2], j // 2 * P, free=False)
                with sp.Fori(1 if base == 0 else 0, NF // 2) as i:
                    for j in range(RING):
                        column_panel(base + j, i, (w_gate, w_up)[j % 2], (2 * i + j // 2) * P)

            def down_panels(base, w):
                for d in range(2):
                    row_panel(base + d, 0, w, d * P)
                with sp.Fori(0, (NF - 2) // RING) as i:
                    for j in range(RING):
                        row_panel(base + 2 + j, i, w, (2 + 4 * i + j) * P)

            up_panels(UP1, ffn1_w_gate, ffn1_w_up)
            down_panels(DOWN1, ffn1_w_down)
            window_q = 3 * W_MOBA
            window_kv = window_q + W_SWA
            for j in range(2):
                column_panel(IN + j, 0, w_in, window_kv + j * P)
            with sp.Fori(0, PAIRS) as i:
                c = IN + 2
                wait_free(c, i)
                for h in range(2):
                    sp.dma_start(raw[:, c % RING, :].rearrange("p (k f) -> p k f", f=P)[:, :, HD * h:HD * h + HD],
                                 w_in[0, :, bass.ds(window_q + (i + 4 * h) * HD, HD)]
                                 .rearrange("(k p) f -> p k f", p=P)).then_inc(raw_loaded[c % RING], 16)
                for j in range(3):
                    column_panel(c + 1 + j, i, w_in, j * W_MOBA + i * P)
            for d in range(D // P):
                row_panel(OUT + d, 0, w_out, d * P)
            up_panels(UP2, ffn2_w_gate, ffn2_w_up)
            down_panels(DOWN2, ffn2_w_down)
            for t in range(NT):
                sp.wait_ge(x_ready, 9 + t)
                sp.dma_start(out[0, t * P:(t + 1) * P, :], xres[:, t, :]).then_inc(out_stored, 16)
            sp.wait_ge(out_stored, 16 * NT)

        @block.gpsimd
        def _(pool):
            def gain(dst, src, done, c0=0, n=D):
                pool.dma_start(dst[:, c0:c0 + n], src.to_broadcast([P, n])).then_inc(done, 16)

            gain(g_a, ffn1_pre_g, gain_a)
            with nc.allow_non_contiguous_dma(reason="64 x 32 bias values"):
                for g in range(2):
                    pool.dma_start(relT[:, g, :], rel_bias[:, 8 * g:8 * g + 8].rearrange("b h -> h b")) \
                        .then_inc(small_loaded, 16)
            pool.dma_start(sinks[:, :], swa_sinks.to_broadcast([P, 8])).then_inc(small_loaded, 16)
            gain(g_b, ffn1_post_g, gain_b)
            gain(g_c, mix_pre_g, gain_c)
            gain(g_d, ffn2_post_g, gain_d)
            nc.gpsimd.memset(expo[:, :], -0.5).then_inc(const_ready, 1)
            nc.gpsimd.memset(ident[:, :], 0.0).then_inc(const_ready, 1)
            pool.wait_ge(const_ready, 2)
            nc.gpsimd.affine_select(out=ident[:, :], in_=ident[:, :], compare_op=ALU.not_equal, fill=1.0, base=0,
                                    pattern=[[-1, P]], channel_multiplier=1).then_inc(ident_ready, 1)

            n_ms = [0]

            def inverse_rms(ss, ms, rs, done, scale):
                eps = EPS * (4 if scale == 4.0 / D else 1)
                nc.gpsimd.tensor_scalar(ms, ss, scale, eps, ALU.mult, ALU.add).then_inc(ms_done, 1)
                n_ms[0] += 1
                pool.wait_ge(ms_done, n_ms[0])
                nc.gpsimd.tensor_tensor(rs, ms, expo[:, 0:ms.shape[1]], ALU.pow).then_inc(done, 1)

            def pre(n, scale=1.0 / D, parts=1):
                pool.wait_ge(ssx_done, sums_of(n))
                inverse_rms(ssx[:, n, 0:parts], msx[:, n, 0:parts], rsx[:, n, 0:parts], rsx_done, scale)

            def post(m, scale):
                pool.wait_ge(ssy_done, m + 1)
                inverse_rms(ssy[:, m:m + 1], msy[:, m:m + 1], rsy[:, m:m + 1], rsy_done, scale)

            for t in range(NT):
                pre(t)

            pool.wait_ge(small_loaded, 48)
            nc.gpsimd.tensor_scalar(nsink[:, :], sinks[:, :], -1.0, None, ALU.mult).then_inc(nsink_ready, 1)
            for b, (first, end) in enumerate(bucket_ranges()):
                nc.gpsimd.tensor_copy(rows[:, :, T - end:T - first],
                                      relT[:, :, b:b + 1].to_broadcast([8, 2, end - first])).then_inc(rows_ready, 1)
            nc.gpsimd.memset(rows[:, :, T:TAB], NEG).then_inc(rows_ready, 1)
            pool.wait_ge(rows_ready, BUCKETS + 1)
            nc.gpsimd.memset(rows[:, 1, 0:T - WINDOW], NEG).then_inc(rows_ready, 1)
            pool.wait_ge(rows_ready, BUCKETS + 2)
            for g in range(2):
                dst = scratch.rearrange("(q g h j) -> h g q j", g=3, h=8, j=TAB)[:, g]
                pool.dma_start(dst, rows[:, g:g + 1, :].to_broadcast([8, P, TAB])).then_inc(rows_stored, 16)

            pool.wait_ge(xn_ready, 4)
            gain(g_a, moba_out_g, gain_a, 0, W_MOBA)
            gain(g_a, swa_out_g, gain_a, W_MOBA, W_SWA)
            for t in range(NT):
                post(t, 4.0 / D)
                pre(4 + t)
            pool.wait_ge(branch_done, 4)
            gain(g_b, mix_post_g, gain_b)
            pool.wait_ge(xn_ready, 8)
            gain(g_c, ffn2_pre_g, gain_c)

            pool.wait_ge(rows_stored, 32)
            pool.wait_ge(nsink_ready, 1)

            def step_operands(i, first):
                if not first:
                    pool.wait_ge(logits_done, 16 * i - 8)
                    pool.wait_ge(exp_done, 16 * i - 8)
                pool.dma_start(bias_s[:, :, :], two_rows(i * TAB + 8 * TAB + T - 2 * P, 4 * TAB, 2 * P)) \
                    .then_inc(bias_s_loaded, 16)
                nc.gpsimd.tensor_copy(nsink_now[:, :], nsink[:, :].rearrange("p (e h) -> p h e", e=2)[:, bass.ds(i, 1), :]
                                      .rearrange("p a e -> p (a e)")).then_inc(sink_ready, 1)
                for parity in range(2):
                    nc.gpsimd.tensor_copy(s_win[:, :, parity, 2 * P:2 * P + 1],
                                          nsink[:, :].rearrange("p (e h) -> p e h", e=2)[:, :, bass.ds(i, 1)]) \
                        .then_inc(sink_ready, 1)
                pool.wait_ge(evac_a, 3 + 3 * i)
                if not first:
                    pool.wait_ge(scores_done, 16 * i - 8)
                    hold_here(pool, pool_held)
                nc.gpsimd.tensor_copy(qs[:, :], qs_next[:, :]).then_inc(qs_ready, 1)
                if not first:
                    pool.wait_ge(logits_done, 16 * i)
                pool.dma_start(bias_m[:, :, :], two_rows(i * (2 * TAB), TAB, T)).then_inc(bias_m_loaded, 16)
                pool.wait_ge(evac_d, 2 + 2 * i)
                if not first:
                    pool.wait_ge(scores_done, 16 * i)
                    hold_here(pool, pool_held)
                nc.gpsimd.tensor_copy(qm[:, :], qm_next[:, :]).then_inc(qk_ready, 1)
                pool.wait_ge(evac_a, 4 + 3 * i)
                if not first:
                    hold_here(pool, pool_held)
                nc.gpsimd.tensor_copy(km[:, :], km_next[:, :]).then_inc(qk_ready, 1)
                pool.wait_ge(evac_a, 5 + 3 * i)
                if not first:
                    pool.wait_ge(pv_done, 16 * i)
                    hold_here(pool, pool_held)
                nc.gpsimd.tensor_copy(vm[:, :, :], vm_next[:, :, :]).then_inc(vm_ready, 1)

            def two_rows(offset, pitch, n):
                return skewed[:, bass.ds(offset, 2 * pitch)].rearrange("q (e r) -> q e r", e=2)[:, :, 0:n]

            step_operands(0, True)
            with pool.Fori(1, PAIRS) as i:
                step_operands(i, False)

            for t in range(NT):
                pre(8 + t, 1.0 / W_MOBA, 2)
            for t in range(NT):
                post(4 + t, 1.0 / D)
                pre(12 + t)
            for t in range(NT):
                post(8 + t, 4.0 / D)

        @block.tensor
        def _(pe):
            def three_passes(dst, a, b, start, stop):
                nc.tensor.matmul(dst, a[0], b[0], start=start, stop=False)
                nc.tensor.matmul(dst, a[0], b[1], start=False, stop=False)
                return nc.tensor.matmul(dst, a[1], b[0], start=False, stop=stop)

            def columns_product(c, bank, ks=range(KD), tokens=slice(0, T)):
                w = stationary_weights(c)
                for k in ks:
                    last = three_passes(ps[:, bank, tokens], [v[:, k, :] for v in w],
                                        [xT_hi[:, k, tokens], xT_lo[:, k, tokens]], k == 0, k == KD - 1)
                return last

            def first_panels(c, banks, n):
                for half in range(2):
                    pe.wait_ge(xT_hi_ready, 2 * (n + 2 * half + 2))
                    pe.wait_ge(xT_lo_ready, 2 * (n + 2 * half + 2))
                    for j in range(RING):
                        if half == 0:
                            wait_split(pe, c + j)
                        last = columns_product(c + j, banks[j], tokens=slice(T // 2 * half, T // 2 * (half + 1)))
                        if half == 1:
                            last.then_inc(panel_used, 1)
                        elif j in (0, 2):
                            transposes(n + 2 + j // 2)

            def up_tile(base, i, t):
                before = 0 if base == UP1 else NF
                pe.wait_ge(h_done, before + 2 * i + t - 1)
                for side in range(2):
                    wait_split(pe, base + 2 * t + side, i)
                    columns_product(base + 2 * t + side, 2 * side + t).then_inc(panel_used, 1)

            def up(base, n):
                first_panels(base, (0, 2, 1, 3), n)
                with pe.Fori(1, NF // 2) as i:
                    for t in range(2):
                        up_tile(base, i, t)

            def row_products(c, act_hi, act_lo, tok, start, stop):
                lhs = [act_hi[:, tok * P:(tok + 1) * P], act_lo[:, tok * P:(tok + 1) * P]]
                for half in range(2):
                    cols = slice(512 * half, 512 * half + 512)
                    last = three_passes(ps[:, 2 * tok + half, :], lhs,
                                        [w_hi[:, c % RING, cols], w_lo[:, c % RING, cols]], start, stop)
                return last

            def down_panel(base, d, i=0, start=False):
                c = base + d
                wait_split(pe, c, i)
                n = (0 if base == DOWN1 else NF) + d + 4 * i + 1
                pe.wait_ge(hs_hi_ready, n)
                pe.wait_ge(hs_lo_ready, n)
                for tok in (2, 3, 0, 1):
                    if start and tok == 0:
                        pe.wait_ge(h_done, NF if base == DOWN1 else 2 * NF)
                    last = row_products(c, hs_hi[:, d % RING, :], hs_lo[:, d % RING, :], tok, start, False)
                last.then_inc(panel_used, 1)

            def transposes(n):
                tok = n % NT
                pe.wait_ge(xn_ready, n + 1)
                for k in range(KD):
                    last = nc.tensor.transpose(ps[:, 2 * tok + k // 4, k % 4 * P:(k % 4 + 1) * P],
                                               xn[:, n % 2, k * P:(k + 1) * P], ident[:, :])
                last.then_inc(xT_in_psum, 1)

            def last_rows(c0, acts, chain):
                for tok in range(NT):
                    for j in range(RING):
                        if tok == 0:
                            wait_split(pe, c0 + j)
                        a_hi, a_lo = acts(j)
                        last = row_products(c0 + j, a_hi, a_lo, tok, False, j == RING - 1)
                        if tok == NT - 1:
                            last.then_inc(panel_used, 1)
                        elif j == RING - 1:
                            last.then_inc(y_done, 1)
                        if chain is not None and tok >= 2 and j == 1:
                            transposes(chain + tok - 2)

            def down(base, chain):
                for d in range(2):
                    down_panel(base, d, start=d == 0)
                with pe.Fori(0, (NF - 2) // RING - 1) as i:
                    for j in range(RING):
                        down_panel(base, 2 + j, i)
                d0 = NF - RING
                pe.wait_ge(hs_hi_ready, NF if base == DOWN1 else 2 * NF)
                pe.wait_ge(hs_lo_ready, NF if base == DOWN1 else 2 * NF)
                last_rows(base + d0, lambda j: (hs_hi[:, (d0 + j) % RING, :], hs_lo[:, (d0 + j) % RING, :]), chain)

            pe.wait_ge(ident_ready, 1)
            for t in range(2):
                transposes(t)
            up(UP1, 0)
            down(DOWN1, 4)

            def values_to_tokens():
                for tok in range(NT):
                    last = nc.tensor.transpose(ps[:, 0, tok * P:(tok + 1) * P], vT[:, tok * P:(tok + 1) * P], ident[:, :])
                last.then_inc(turned_values, 1)

            def project_next(i, k):
                j = k // 4
                if j < 4:
                    if k % 4 == 0:
                        if j % 2 == 0:
                            pe.wait_ge(evac_a, 2 + 3 * i + j // 2)
                        else:
                            pe.wait_ge(evac_d, 1 + 2 * i + j // 2)
                        wait_split(pe, IN + 2 + j, i)
                    last = columns_product(IN + 2 + j, j % 2, [2 * (k % 4), 2 * (k % 4) + 1])
                    if k % 4 == 3:
                        last.then_inc(panel_used, 1)
                elif k == 17:
                    pe.wait_ge(evac_a, 4 + 3 * i)
                    pe.wait_ge(evac_d, 3 + 2 * i)
                    values_to_tokens()

            def scores(i, k):
                win, e, qt, kts = unit(k)
                g = UNITS * i + k
                if k == 0:
                    pe.wait_ge(qs_ready, i + 1)
                if k == 8:
                    pe.wait_ge(qk_ready, 2 * (i + 1))
                if k >= 2:
                    pe.wait_ge(logits_done, g - 1)
                elif not isinstance(i, int):
                    pe.wait_ge(logits_done, g - 1)
                elif g >= 2:
                    pe.wait_ge(logits_done, g - 1)
                q, kk = (qs, ksT) if win else (qm, km)
                rows_ = slice(HD * e, HD * e + HD)
                nc.tensor.matmul(ps[:, 2 + k % 2, 0:len(kts) * P], q[rows_, qt * P:(qt + 1) * P],
                                 kk[rows_, kts[0] * P:(kts[-1] + 1) * P], start=True, stop=True).then_inc(scores_done, 1)

            def turn(i, k, first):
                win, e, qt, kts = unit(k)
                g = UNITS * i + k
                pe.wait_ge(exp_done, g + 1)
                if k >= 2 or not first:
                    pe.wait_ge(pT_by_act if k % 2 == 0 else pT_by_dve, 8 * i + k // 2)
                for n in range(len(kts)):
                    last = nc.tensor.transpose(ps[:, 4 + k % 2, n * P:(n + 1) * P], prob[:, k % RING, n * P:(n + 1) * P],
                                               ident[:, :])
                last.then_inc(pT_in_psum, 1)

            def values(i, k, first):
                win, e, qt, kts = unit(k)
                pe.wait_ge(pT_by_act if k % 2 == 0 else pT_by_dve, 8 * i + k // 2 + 1)
                if qt == 0 and (k >= 8 or not first):
                    pe.wait_ge(att_done, 4 * i + k // 4 - 1)
                if k == 8:
                    pe.wait_ge(vm_ready, i + 1)
                v = vs if win else vm
                for n, kt in enumerate(kts):
                    last = nc.tensor.matmul(ps[:, 6 + k // 4 % 2, qt * HD:(qt + 1) * HD], pT[:, k % 2, n * P:(n + 1) * P],
                                            v[:, kt, HD * e:HD * e + HD], start=n == 0, stop=n == len(kts) - 1)
                last.then_inc(pv_done, 1)

            first_panels(IN, (0, 1, 2, 3), 4)
            pe.wait_ge(evac_a, 1)
            pe.wait_ge(evac_d, 1)
            values_to_tokens()
            pe.wait_ge(evac_a, 2)
            wait_split(pe, IN + 4)
            columns_product(IN + 4, 0).then_inc(panel_used, 1)
            wait_split(pe, IN + 5)
            columns_product(IN + 5, 1).then_inc(panel_used, 1)
            project_next(0, 17)

            def attention(i, first, following):
                for k in range(STEPS):
                    if k < UNITS:
                        scores(i, k)
                    if 2 <= k < UNITS + 2:
                        turn(i, k - 2, first)
                    if k >= 3:
                        values(i, k - 3, first)
                    if following:
                        project_next(i + 1, k)

            attention(0, True, True)
            with pe.Fori(1, PAIRS - 1) as i:
                attention(i, False, True)
            attention(PAIRS - 1, False, False)

            for t in range(2):
                transposes(8 + t)
            for d in range(D // P - RING):
                wait_split(pe, OUT + d)
                for tok in range(NT):
                    if d == 0:
                        pe.wait_ge(xT_hi_ready, 2 * (8 + tok + 1))
                        pe.wait_ge(xT_lo_ready, 2 * (8 + tok + 1))
                        if tok < 2:
                            transposes(8 + tok + 2)
                    last = row_products(OUT + d, xT_hi[:, d, :], xT_lo[:, d, :], tok, d == 0, False)
                last.then_inc(panel_used, 1)
            d0 = D // P - RING
            last_rows(OUT + d0, lambda j: (xT_hi[:, d0 + j, :], xT_lo[:, d0 + j, :]), 12)
            up(UP2, 12)
            down(DOWN2, None)

        @block.scalar
        def _(act):
            def split_hi(c, i=0, first=False):
                wait_loaded(act, c, i)
                if not first:
                    act.wait_ge(panel_used, c + 4 * i - RING + 1)
                nc.scalar.activation(w_hi[:, c % RING, :], raw[:, c % RING, :], ACT.Copy).then_inc(hi_ready, 1)

            squares = []

            def square_sum(src, dst, done, count):
                if len(squares) >= 2:
                    act.wait_ge(*squares[-2])
                nc.scalar.activation(junk[:, len(squares) % 2, 0:src.shape[1]], src, ACT.Square, accum_out=dst) \
                    .then_inc(done, 1)
                squares.append((done, count))

            def sum_y(m):
                if m % NT < NT - 1:
                    act.wait_ge(y_done, (NT - 1) * (m // NT) + m % NT + 1)
                else:
                    act.wait_ge(panel_used, (DOWN1 + NF, OUT + D // P, DOWN2 + NF)[m // NT])
                square_sum(bank2(m % NT), ssy[:, m:m + 1], ssy_done, m + 1)

            def sum_x(n, y=None):
                if y is not None:
                    act.wait_ge(x_ready, y + 1)
                square_sum(xres[:, n % NT, :], ssx[:, n, 0:1], ssx_done, sums_of(n))

            def turned_hi(n):
                tok = n % NT
                act.wait_ge(xT_in_psum, n + 1)
                for b in range(2):
                    nc.scalar.activation(xT_hi[:, 4 * b:4 * b + 4, tok * P:(tok + 1) * P],
                                         ps[:, 2 * tok + b, :].rearrange("p (k t) -> p k t", t=P), ACT.Copy) \
                        .then_inc(xT_hi_ready, 1)

            def silu(base, i, t):
                n = (0 if base == UP1 else NF) + 2 * i + t
                act.wait_ge(panel_used, base + 4 * i + 2 * t + 1)
                if not isinstance(i, int) or base == UP2:
                    act.wait_ge(h_done, n - 1)
                nc.scalar.activation(tmp[:, 512 * t:512 * t + 512], ps[:, t, :], ACT.Silu).then_inc(silu_done, 1)

            def up(base, down_base):
                for t in range(2):
                    split_hi(base + RING + t)
                    silu(base, 0, t)
                for d in range(2):
                    stage_hidden(down_base, d)
                with act.Fori(1, NF // 2) as i:
                    for t in range(2):
                        for side in range(2):
                            split_hi(base + 2 * t + side + LEAD, i)
                        silu(base, i, t)

            def stage_hidden(base, d, i=0):
                if d >= RING or not isinstance(i, int):
                    act.wait_ge(panel_used, base + d + 4 * i - RING + 1)
                act.wait_ge(h_done, (0 if base == DOWN1 else NF) + d + 4 * i + 1)
                nc.scalar.activation(hs_hi[:, d % RING, :], hT[:, bass.ds(d + 4 * i, 1), :].rearrange("p a t -> p (a t)"),
                                     ACT.Copy).then_inc(hs_hi_ready, 1)

            def down(base, chain):
                for d in range(2):
                    split_hi(base + d + LEAD)
                    stage_hidden(base, d + LEAD)
                with act.Fori(0, (NF - 2) // RING - 1) as i:
                    for j in range(RING):
                        split_hi(base + 2 + j + LEAD, i)
                        stage_hidden(base, 2 + j + LEAD, i)
                for d in range(NF - RING, NF - LEAD):
                    split_hi(base + d + LEAD)
                    stage_hidden(base, d + LEAD)

            def norms(m, n, following):
                for t in range(2):
                    sum_y(m + t)
                    sum_x(n + t, m + t)
                turned_hi(n)
                sum_y(m + 2)
                split_hi(following)
                turned_hi(n + 1)
                split_hi(following + 1)
                sum_x(n + 2, m + 2)
                sum_y(m + 3)
                split_hi(following + 2)
                turned_hi(n + 2)
                sum_x(n + 3, m + 3)
                split_hi(following + 3)
                turned_hi(n + 3)

            for t in range(NT):
                act.wait_ge(x_loaded[t], 16)
                sum_x(t)
                if t >= 1:
                    turned_hi(t - 1)
                split_hi(t, first=True)
            turned_hi(NT - 1)
            up(UP1, DOWN1)
            down(DOWN1, 4)
            norms(0, 4, IN)

            def evacuate(dst, n, scale=1.0, done=panel_used, bank=0):
                act.wait_ge(done, n)
                nc.scalar.activation(dst, ps[:, bank, :], ACT.Copy, scale=scale).then_inc(evac_a, 1)

            def project_next(i, k):
                if k < UNITS and k % 4 == 1:
                    j = k // 4 + LEAD
                    split_hi(IN + 2 + j, i)
                if k == 4:
                    if not isinstance(i, int) or i > 0:
                        act.wait_ge(qs_ready, i)
                    evacuate(qs_next[:, :], IN + 2 + 4 * i + 1, SCALE)
                if k == 12:
                    if not isinstance(i, int) or i > 0:
                        act.wait_ge(qk_ready, 2 * i)
                    evacuate(km_next[:, :], IN + 2 + 4 * i + 3)
                if k == 18:
                    if not isinstance(i, int) or i > 0:
                        act.wait_ge(vm_ready, i)
                    evacuate(vm_next[:, :, :].rearrange("p t c -> p (t c)"), i + 2, done=turned_values)

            def exponent(i, k, first):
                win, e, qt, kts = unit(k)
                g = UNITS * i + k
                act.wait_ge(logits_done, g + 1)
                if k >= RING or not first:
                    act.wait_ge(pT_in_psum, g - RING + 1)
                if k % 4 == 0 and not first:
                    act.wait_ge(att_done, 4 * i + k // 4 - 3)
                if k == 0:
                    act.wait_ge(sink_ready, 3 * (i + 1))
                n = len(kts) * P
                src = s_win[:, e, k % 2, 2 * P - n:2 * P + 1] if win else s_moba[:, k % 2, 0:n]
                nc.scalar.activation(prob[:, k % RING, 0:n + win], src, ACT.Exp, scale=-1.0, bias=nmax[:, k:k + 1],
                                     accum_out=psumrow[:, k:k + 1]).then_inc(exp_done, 1)

            def evacuate_turned(i, k, first):
                if k % 2:
                    return
                n = len(unit(k)[3]) * P
                act.wait_ge(pT_in_psum, UNITS * i + k + 1)
                if k >= 2 or not first:
                    act.wait_ge(pv_done, UNITS * i + k - 1)
                nc.scalar.activation(pT[:, 0, 0:n], ps[:, 4, 0:n], ACT.Copy).then_inc(pT_by_act, 1)

            evacuate(ksT[:, :], IN + 1)
            split_hi(IN + 4)
            split_hi(IN + 5)
            evacuate(vs[:, :, :].rearrange("p t c -> p (t c)"), 1, done=turned_values)
            evacuate(qs_next[:, :], IN + 3, SCALE, bank=2)
            split_hi(IN + 6)
            split_hi(IN + 7)
            evacuate(km_next[:, :], IN + 6)
            project_next(0, 18)

            def attention(i, first, following):
                for k in range(STEPS):
                    if k < UNITS:
                        exponent(i, k, first)
                    if 2 <= k < UNITS + 2:
                        evacuate_turned(i, k - 2, first)
                    if following:
                        project_next(i + 1, k)

            attention(0, True, True)
            with act.Fori(1, PAIRS - 1) as i:
                attention(i, False, True)
            attention(PAIRS - 1, False, False)

            act.wait_ge(att_done, 4 * PAIRS)
            for t in range(NT):
                for g in range(2):
                    square_sum(att[:, t, 512 * g:512 * g + 512], ssx[:, 8 + t, g:g + 1], ssx_done,
                               sums_of(8 + t) + g - 1)
                if t >= 1:
                    turned_hi(8 + t - 1)
            turned_hi(8 + NT - 1)
            for d in range(D // P - LEAD):
                split_hi(OUT + d + LEAD)
            norms(4, 12, UP2)
            up(UP2, DOWN2)
            down(DOWN2, None)
            for t in range(NT):
                sum_y(8 + t)

        @block.vector
        def _(dve):
            def split_lo(c, i=0):
                dve.wait_ge(hi_ready, c + 4 * i + 1)
                nc.vector.tensor_tensor(w_lo[:, c % RING, :], raw[:, c % RING, :], w_hi[:, c % RING, :].bitcast(F32),
                                        ALU.subtract).then_inc(lo_ready, 1)

            def branch(m, g):
                dve.wait_ge(rsy_done, m + 1)
                if m % NT:
                    dve.wait_ge(x_ready, m)
                nc.vector.scalar_tensor_tensor(out=tmp[:, :], in0=bank2(m % NT), scalar=rsy[:, m:m + 1], in1=g[:, :],
                                               op0=ALU.mult, op1=ALU.mult).then_inc(branch_done, 1)

            def residual(m):
                dve.wait_ge(branch_done, m + 1)
                nc.vector.tensor_tensor(xres[:, m % NT, :], xres[:, m % NT, :], tmp[:, :], ALU.add).then_inc(x_ready, 1)

            def normalise(n, g):
                dve.wait_ge(rsx_done, n + 1)
                if n >= 2:
                    dve.wait_ge(xT_in_psum, n - 1)
                nc.vector.scalar_tensor_tensor(out=xn[:, n % 2, :], in0=xres[:, n % NT, :], scalar=rsx[:, n, 0:1],
                                               in1=g[:, :], op0=ALU.mult, op1=ALU.mult).then_inc(xn_ready, 1)

            def turned_lo(n):
                tok = n % NT
                for b in range(2):
                    dve.wait_ge(xT_hi_ready, 2 * n + b + 1)
                    span = (slice(None), slice(4 * b, 4 * b + 4), slice(tok * P, (tok + 1) * P))
                    nc.vector.tensor_tensor(xT_lo[span], ps[:, 2 * tok + b, :].rearrange("p (k t) -> p k t", t=P),
                                            xT_hi[span].bitcast(F32), ALU.subtract).then_inc(xT_lo_ready, 1)

            def hidden(base, i, t):
                n = (0 if base == UP1 else NF) + 2 * i + t
                dve.wait_ge(silu_done, n + 1)
                dve.wait_ge(panel_used, base + 4 * i + 2 * t + 2)
                nc.vector.tensor_tensor(hT[:, bass.ds(2 * i + t, 1), :].rearrange("p a t -> p (a t)"),
                                        ps[:, 2 + t, :], tmp[:, 512 * t:512 * t + 512], ALU.mult).then_inc(h_done, 1)

            def up(base, down_base):
                for t in range(2):
                    split_lo(base + RING + t)
                    hidden(base, 0, t)
                for d in range(2):
                    stage_hidden(down_base, d)
                with dve.Fori(1, NF // 2) as i:
                    for t in range(2):
                        for side in range(2):
                            split_lo(base + 2 * t + side + LEAD, i)
                        hidden(base, i, t)

            def stage_hidden(base, d, i=0):
                dve.wait_ge(hs_hi_ready, (0 if base == DOWN1 else NF) + d + 4 * i + 1)
                nc.vector.tensor_tensor(hs_lo[:, d % RING, :], hT[:, bass.ds(d + 4 * i, 1), :].rearrange("p a t -> p (a t)"),
                                        hs_hi[:, d % RING, :].bitcast(F32), ALU.subtract).then_inc(hs_lo_ready, 1)

            def down(base):
                for d in range(2):
                    split_lo(base + d + LEAD)
                    stage_hidden(base, d + LEAD)
                with dve.Fori(0, (NF - 2) // RING - 1) as i:
                    for j in range(RING):
                        split_lo(base + 2 + j + LEAD, i)
                        stage_hidden(base, 2 + j + LEAD, i)
                for d in range(NF - RING, NF - LEAD):
                    split_lo(base + d + LEAD)
                    stage_hidden(base, d + LEAD)

            def norms(m, n, g_post, g_pre, following):
                for t in range(2):
                    branch(m + t, g_post)
                    residual(m + t)
                    normalise(n + t, g_pre)
                turned_lo(n)
                branch(m + 2, g_post)
                split_lo(following)
                residual(m + 2)
                turned_lo(n + 1)
                split_lo(following + 1)
                normalise(n + 2, g_pre)
                branch(m + 3, g_post)
                residual(m + 3)
                split_lo(following + 2)
                turned_lo(n + 2)
                normalise(n + 3, g_pre)
                split_lo(following + 3)
                turned_lo(n + 3)

            dve.wait_ge(gain_a, 16)
            for t in range(NT):
                normalise(t, g_a)
                if t >= 1:
                    turned_lo(t - 1)
                split_lo(t)
            turned_lo(NT - 1)
            up(UP1, DOWN1)
            down(DOWN1)
            dve.wait_ge(gain_b, 16)
            dve.wait_ge(gain_c, 16)
            norms(0, 4, g_b, g_c, IN)

            def evacuate(dst, n, scale=1.0, bank=1):
                dve.wait_ge(panel_used, n)
                nc.vector.tensor_scalar(dst, ps[:, bank, :], scale, None, ALU.mult).then_inc(evac_d, 1)

            def project_next(i, k):
                if k < UNITS and k % 4 == 1:
                    split_lo(IN + 2 + k // 4 + LEAD, i)
                if k == 8:
                    if not isinstance(i, int) or i > 0:
                        dve.wait_ge(qk_ready, 2 * i)
                    evacuate(qm_next[:, :], IN + 2 + 4 * i + 2, SCALE)
                if k == 16:
                    evacuate(vT[:, :], IN + 2 + 4 * i + 4)

            def logits(i, k, first):
                win, e, qt, kts = unit(k)
                g = UNITS * i + k
                dve.wait_ge(scores_done, g + 1)
                if k >= 2 or not first:
                    dve.wait_ge(exp_done, g - 1)
                n = len(kts) * P
                if k == 0:
                    dve.wait_ge(bias_s_loaded, 16 * (i + 1))
                    dve.wait_ge(sink_ready, 3 * (i + 1))
                if k == 8:
                    dve.wait_ge(bias_m_loaded, 16 * (i + 1))
                if not isinstance(i, int):
                    hold_here(dve, dve_held)
                nc.vector.tensor_tensor_reduce(
                    out=s_win[:, e, k % 2, 2 * P - n:2 * P] if win else s_moba[:, k % 2, 0:n],
                    in0=ps[:, 2 + k % 2, 0:n], in1=bias_s[:, e, 2 * P - n:2 * P] if win else bias_m[:, e, T - n:T],
                    scale=-1.0, scalar=nsink_now[:, e:e + 1] if win else BIG, op0=ALU.add, op1=ALU.min,
                    accum_out=nmax[:, k:k + 1]).then_inc(logits_done, 1)

            def evacuate_turned(i, k, first):
                if k % 2 == 0:
                    return
                n = len(unit(k)[3]) * P
                dve.wait_ge(pT_in_psum, UNITS * i + k + 1)
                if k >= 2 or not first:
                    dve.wait_ge(pv_done, UNITS * i + k - 1)
                nc.vector.tensor_copy(pT[:, 1, 0:n], ps[:, 5, 0:n]).then_inc(pT_by_dve, 1)

            def head_done(i, h):
                g = 4 * i + h
                win, e = h < 2, h % 2
                dve.wait_ge(pv_done, 4 * (g + 1))
                dve.wait_ge(exp_done, 4 * (g + 1))
                nc.vector.reciprocal(rinv[:, 4 * h:4 * h + 4], psumrow[:, 4 * h:4 * h + 4]).then_inc(rinv_done, 1)
                dve.wait_ge(rinv_done, g + 1)
                col = W_MOBA + (i + 4 * e) * HD if win else (2 * i + e) * HD
                nc.vector.tensor_tensor(att[:, :, bass.ds(col, HD)],
                                        ps[:, 6 + e, 0:4 * HD].rearrange("p (t c) -> p t c", c=HD),
                                        rinv[:, 4 * h:4 * h + 4].rearrange("p (t a) -> p t a", a=1)
                                        .to_broadcast([P, NT, HD]), ALU.mult).then_inc(att_done, 1)

            evacuate(vT[:, :], IN + 2)
            split_lo(IN + 4)
            split_lo(IN + 5)
            evacuate(qm_next[:, :], IN + 4, SCALE, bank=3)
            split_lo(IN + 6)
            split_lo(IN + 7)
            project_next(0, 16)

            def attention(i, first, following):
                for k in range(STEPS):
                    if k < UNITS:
                        logits(i, k, first)
                    if 2 <= k < UNITS + 2:
                        evacuate_turned(i, k - 2, first)
                    if k >= 7 and (k - 7) % 4 == 0:
                        head_done(i, (k - 7) // 4)
                    if following:
                        project_next(i + 1, k)
                head_done(i, 3)

            attention(0, True, True)
            with dve.Fori(1, PAIRS - 1) as i:
                attention(i, False, True)
            attention(PAIRS - 1, False, False)

            def normalise_att(n):
                tok = n % NT
                dve.wait_ge(rsx_done, n + 1)
                dve.wait_ge(xT_in_psum, n - 1)
                for g in range(2):
                    cols = slice(512 * g, 512 * g + 512)
                    last = nc.vector.scalar_tensor_tensor(out=xn[:, n % 2, cols], in0=att[:, tok, cols],
                                                          scalar=rsx[:, n, g:g + 1], in1=g_a[:, cols],
                                                          op0=ALU.mult, op1=ALU.mult)
                last.then_inc(xn_ready, 1)

            dve.wait_ge(gain_a, 48)
            for t in range(NT):
                normalise_att(8 + t)
                if t >= 1:
                    turned_lo(8 + t - 1)
            turned_lo(8 + NT - 1)
            for d in range(D // P - LEAD):
                split_lo(OUT + d + LEAD)
            dve.wait_ge(gain_b, 32)
            dve.wait_ge(gain_c, 32)
            norms(4, 12, g_b, g_c, UP2)
            up(UP2, DOWN2)
            down(DOWN2)
            dve.wait_ge(gain_d, 16)
            for t in range(NT):
                branch(8 + t, g_d)
                residual(8 + t)


_INS = ['x', 'ffn1_pre_g', 'ffn1_w_gate', 'ffn1_w_up', 'ffn1_w_down', 'ffn1_post_g', 'mix_pre_g', 'w_in', 'rel_bias',
        'moba_out_g', 'swa_sinks', 'swa_out_g', 'w_out', 'mix_post_g', 'ffn2_pre_g', 'ffn2_w_gate', 'ffn2_w_up',
        'ffn2_w_down', 'ffn2_post_g']
_OUTS = [((1, T, D), 'float32')]


def kernel(**inputs):
    import numpy as _np
    import concourse.bacc as _bacc
    from concourse import mybir as _mybir
    from concourse.bass_utils import run_bass_kernel_spmd as _run

    nc = _bacc.Bacc("TRN2", target_bir_lowering=False, num_devices=1)
    arrays, args = {}, []
    for name in _INS:
        a = _np.ascontiguousarray(inputs[name])
        arrays[f"in_{name}_dram"] = a
        args.append(nc.dram_tensor(f"in_{name}_dram", a.shape, _mybir.dt.from_np(a.dtype), kind="ExternalInput").ap())
    for i, (shape, dtype) in enumerate(_OUTS):
        dt = _mybir.dt.from_np(_np.dtype(dtype))
        args.append(nc.dram_tensor(f"out_{i}_dram", shape, dt, kind="ExternalOutput").ap())
    build(nc, *args)
    r = _run(nc, [arrays], core_ids=[0])
    got = tuple(r.results[0][f"out_{i}_dram"] for i in range(len(_OUTS)))
    return got[0]
```

```python
import math
from contextlib import ExitStack

import numpy as np
import concourse.bass as bass
from concourse import mybir

ALU = mybir.AluOpType
ACT = mybir.ActivationFunctionType
F32 = mybir.dt.float32
F32R = mybir.dt.float32r
BF16 = mybir.dt.bfloat16

P = 128
D = 1024
T = 512
F = 2816
KD = D // P
NT = T // P
NF = F // P
HD = 64
W_MOBA = 512
W_SWA = 512
BUCKETS = 32
MAX_DISTANCE = 128
WINDOW = 128
EPS = 1e-6
NEG = -1e30
BIG = 3.0e38
SCALE = HD ** -0.5

RING = 4
UP1 = 0
DOWN1 = UP1 + 2 * NF
IN = DOWN1 + NF
OUT = IN + 18
UP2 = OUT + D // P
DOWN2 = UP2 + 2 * NF
PANELS = DOWN2 + NF
LEAD = 2

PAIRS = 4
UNITS = 16
DRAIN = 3
TAB = 640


def bucket_ranges():
    exact = BUCKETS // 2

    def bucket(n):
        if n < exact:
            return n
        large = exact + int(np.float32(np.log(np.float32(n) / np.float32(exact)) / np.float32(math.log(MAX_DISTANCE / exact)))
                            * np.float32(BUCKETS - exact))
        return min(large, BUCKETS - 1)

    of = [bucket(n) for n in range(T)]
    return [(of.index(b), T - of[::-1].index(b)) for b in range(BUCKETS)]


def build(nc, x, ffn1_pre_g, ffn1_w_gate, ffn1_w_up, ffn1_w_down, ffn1_post_g, mix_pre_g, w_in, rel_bias,
          moba_out_g, swa_sinks, swa_out_g, w_out, mix_post_g, ffn2_pre_g, ffn2_w_gate, ffn2_w_up,
          ffn2_w_down, ffn2_post_g, out):
    ctx = ExitStack()
    with ctx:
        def sb(name, shape, dt=F32, scope=ctx):
            return scope.enter_context(nc.sbuf_tensor(name, shape, dt))

        def sem(name):
            return ctx.enter_context(nc.semaphore(name))

        ps = ctx.enter_context(nc.psum_tensor("ps", [P, 8, 512], F32))
        xres = sb("xres", [P, NT, D])
        xT_hi = sb("xT_hi", [P, KD, T], F32R)
        xT_lo = sb("xT_lo", [P, KD, T], F32R)
        raw = sb("raw", [P, RING, 1024])
        w_hi = sb("w_hi", [P, RING, 1024], F32R)
        w_lo = sb("w_lo", [P, RING, 1024], F32R)
        g_a = sb("g_a", [P, D])
        g_b = sb("g_b", [P, D])
        g_c = sb("g_c", [P, D])
        g_d = sb("g_d", [P, D])
        xn = sb("xn", [P, 2, D])
        tmp = sb("tmp", [P, D])
        junk = sb("junk", [P, 2, D], BF16)
        ident = sb("ident", [P, P])
        expo = sb("expo", [P, 2])
        ssy = sb("ssy", [P, 12])
        msy = sb("msy", [P, 12])
        rsy = sb("rsy", [P, 12])
        ssx = sb("ssx", [P, 12])
        msx = sb("msx", [P, 12])
        rsx = sb("rsx", [P, 12])
        ssa = sb("ssa", [P, 2 * NT])
        msa = sb("msa", [P, 2 * NT])
        rsa = sb("rsa", [P, 2 * NT])
        sinks = sb("sinks", [P, 8])
        nsink = sb("nsink", [P, 8])
        relT = sb("relT", [8, 2, BUCKETS])
        rows = sb("rows", [8, 2, TAB])
        with ExitStack() as only_ffn:
            hT = sb("hT", [P, NF, T], F32, only_ffn)
            hs_hi = sb("hs_hi", [P, RING, T], F32R, only_ffn)
            hs_lo = sb("hs_lo", [P, RING, T], F32R, only_ffn)
        ksT = sb("ksT", [P, T])
        vs = sb("vs", [P, NT, P])
        vT = sb("vT", [P, T])
        qs, qm, km = sb("qs", [P, T]), sb("qm", [P, T]), sb("km", [P, T])
        vm = sb("vm", [P, NT, P])
        bias_s = sb("bias_s", [P, 2, 2 * P])
        bias_m = sb("bias_m", [P, 2, T])
        nsink_now = sb("nsink_now", [P, 2])
        s_win = sb("s_win", [P, 2, 2, 2 * P + 1])
        s_moba = sb("s_moba", [P, 2, T])
        prob = sb("prob", [P, RING, T + 2])
        pT = sb("pT", [P, 2, T])
        nmax = sb("nmax", [P, UNITS])
        psumrow = sb("psumrow", [P, UNITS])
        rinv = sb("rinv", [P, UNITS])
        att = sb("att", [P, NT, D])

        PITCH = 24 * TAB
        scratch = nc.dram_tensor("bias_rows", (P * PITCH,), F32, kind="Internal").ap()
        skewed = scratch[P - 1:P - 1 + P * (PITCH - 1)].rearrange("(q r) -> q r", r=PITCH - 1)

        x_loaded = [sem(f"x_loaded{t}") for t in range(NT)]
        gain_a, gain_b, gain_c, gain_d = sem("gain_a"), sem("gain_b"), sem("gain_c"), sem("gain_d")
        small_loaded = sem("small_loaded")
        raw_loaded = [sem(f"raw_loaded{s}") for s in range(RING)]
        hi_ready, lo_ready, panel_used = sem("hi_ready"), sem("lo_ready"), sem("panel_used")
        silu_done, h_done = sem("silu_done"), sem("h_done")
        hs_hi_ready, hs_lo_ready = sem("hs_hi_ready"), sem("hs_lo_ready")
        y_done, ssy_done, rsy_done = sem("y_done"), sem("ssy_done"), sem("rsy_done")
        branch_done, x_ready = sem("branch_done"), sem("x_ready")
        ssx_done, rsx_done, xn_ready = sem("ssx_done"), sem("rsx_done"), sem("xn_ready")
        xT_in_psum, xT_hi_ready, xT_lo_ready = sem("xT_in_psum"), sem("xT_hi_ready"), sem("xT_lo_ready")
        const_ready, pool_step, ident_ready = sem("const_ready"), sem("pool_step"), sem("ident_ready")
        ms_done = sem("ms_done")
        rows_ready, rows_stored = sem("rows_ready"), sem("rows_stored")
        nsink_ready = sem("nsink_ready")
        ks_ready, vs_ready, vT_ready, turned_values = sem("ks_ready"), sem("vs_ready"), sem("vT_ready"), sem("turned_values")
        qs_ready, qm_ready, km_ready, vm_ready = sem("qs_ready"), sem("qm_ready"), sem("km_ready"), sem("vm_ready")
        bias_s_loaded, bias_m_loaded, sink_ready = sem("bias_s_loaded"), sem("bias_m_loaded"), sem("sink_ready")
        scores_done, logits_done, exp_done = sem("scores_done"), sem("logits_done"), sem("exp_done")
        pT_in_psum, pT_by_act, pT_by_dve = sem("pT_in_psum"), sem("pT_by_act"), sem("pT_by_dve")
        pv_done, rinv_done, att_done = sem("pv_done"), sem("rinv_done"), sem("att_done")
        ssa_done, rsa_done, an_ready = sem("ssa_done"), sem("rsa_done"), sem("an_ready")
        aT_in_psum, aT_hi_ready, aT_lo_ready = sem("aT_in_psum"), sem("aT_hi_ready"), sem("aT_lo_ready")
        out_stored = sem("out_stored")
        dve_held = sem("dve_held")

        def bank2(tok):
            return ps[:, 2 * tok:2 * tok + 2, :].rearrange("p b n -> p (b n)")

        def att_cols(h):
            return slice(W_MOBA, D) if h < NT else slice(0, W_MOBA)

        def att_bank(h):
            return 1 if h < NT else 6 + h % 2

        def unit(k):
            win, e, qt = k < 8, k // 4 % 2, k % 4
            return win, e, qt, list(range(max(qt - 1, 0), qt + 1)) if win else list(range(qt + 1))

        def lagging(i, k, lag):
            return (i, k - lag) if k >= lag else (i - 1, k - lag + UNITS)

        def has_lagging(k, lag, first):
            return k - lag < UNITS and (k >= lag or not first)

        def wait_loaded(eng, c, i=0):
            n = c // RING + i + 1
            if c % RING == 0 and c >= IN:
                n = n + (c // RING + i - IN // RING if c < UP2 else UP2 // RING - 1 - IN // RING)
            eng.wait_ge(raw_loaded[c % RING], 16 * n)

        def wait_split(eng, c, i=0):
            eng.wait_ge(hi_ready, c + 4 * i + 1)
            eng.wait_ge(lo_ready, c + 4 * i + 1)

        def stationary_weights(c):
            return [w[:, c % RING, :].rearrange("p (k f) -> p k f", f=P) for w in (w_hi, w_lo)]

        block = ctx.enter_context(nc.Block())

        def hold_here(eng, counter):
            eng.sem_inc(counter, 1)

        @block.sync
        def _(sp):
            def load_x(t):
                sp.dma_start(xres[:, t, :], x[0, t * P:(t + 1) * P, :]).then_inc(x_loaded[t], 16)

            def wait_free(c, i):
                sp.wait_ge(lo_ready, c + 4 * i - RING + 1)

            def column_panel(c, i, w, col, free=True):
                if free:
                    wait_free(c, i)
                sp.dma_start(raw[:, c % RING, :].rearrange("p (k f) -> p k f", f=P),
                             w[0, :, bass.ds(col, P)].rearrange("(k p) f -> p k f", p=P)) \
                    .then_inc(raw_loaded[c % RING], 16)

            def row_panel(c, i, w, row):
                wait_free(c, i)
                parts = 2 if c % RING == 0 and IN <= c < UP2 else 1
                for n in range(parts):
                    cols = slice(n * (D // parts), (n + 1) * (D // parts))
                    sp.dma_start(raw[:, c % RING, cols], w[0, bass.ds(row, P), cols]).then_inc(raw_loaded[c % RING], 16)

            def up_panels(base, w_gate, w_up):
                if base == 0:
                    for j in range(RING):
                        load_x(j)
                        if j % 2 == 0:
                            continue
                        for p in (j - 1, j):
                            column_panel(p, 0, (w_gate, w_up)[p % 2], p // 2 * P, free=False)
                with sp.Fori(1 if base == 0 else 0, NF // 2) as i:
                    for j in range(RING):
                        column_panel(base + j, i, (w_gate, w_up)[j % 2], (2 * i + j // 2) * P)

            def down_panels(base, w):
                for d in range(2):
                    row_panel(base + d, 0, w, d * P)
                with sp.Fori(0, (NF - 2) // RING) as i:
                    for j in range(RING):
                        row_panel(base + 2 + j, i, w, (2 + 4 * i + j) * P)

            up_panels(UP1, ffn1_w_gate, ffn1_w_up)
            down_panels(DOWN1, ffn1_w_down)
            window_q = 3 * W_MOBA
            window_kv = window_q + W_SWA
            for j in range(2):
                column_panel(IN + j, 0, w_in, window_kv + j * P)
            with sp.Fori(0, PAIRS) as i:
                c = IN + 2
                wait_free(c, i)
                for h in range(2):
                    sp.dma_start(raw[:, c % RING, :].rearrange("p (k f) -> p k f", f=P)[:, :, HD * h:HD * h + HD],
                                 w_in[0, :, bass.ds(window_q + (i + 4 * h) * HD, HD)]
                                 .rearrange("(k p) f -> p k f", p=P)).then_inc(raw_loaded[c % RING], 16)
                for j in range(3):
                    column_panel(c + 1 + j, i, w_in, j * W_MOBA + i * P)
            for d in range(D // P):
                row_panel(OUT + d, 0, w_out, (d + W_MOBA // P) * P % D)
            up_panels(UP2, ffn2_w_gate, ffn2_w_up)
            down_panels(DOWN2, ffn2_w_down)
            for t in range(NT):
                sp.wait_ge(x_ready, 9 + t)
                sp.dma_start(out[0, t * P:(t + 1) * P, :], xres[:, t, :]).then_inc(out_stored, 16)
            sp.wait_ge(out_stored, 16 * NT)

        @block.gpsimd
        def _(pool):
            def gain(dst, src, done, c0=0, n=D):
                pool.dma_start(dst[:, c0:c0 + n], src.to_broadcast([P, n])).then_inc(done, 16)

            gain(g_a, ffn1_pre_g, gain_a)
            nc.gpsimd.memset(expo[:, :], -0.5).then_inc(const_ready, 1)
            nc.gpsimd.memset(ident[:, :], 0.0).then_inc(const_ready, 1)
            pool.wait_ge(const_ready, 2)
            nc.gpsimd.affine_select(out=ident[:, :], in_=ident[:, :], compare_op=ALU.not_equal, fill=1.0, base=0,
                                    pattern=[[-1, P]], channel_multiplier=1).then_inc(ident_ready, 1)

            n_ms = [0]

            def inverse_rms(ss, ms, rs, done, scale):
                eps = EPS * (4 if scale == 4.0 / D else 1)
                nc.gpsimd.tensor_scalar(ms, ss, scale, eps, ALU.mult, ALU.add).then_inc(ms_done, 1)
                n_ms[0] += 1
                pool.wait_ge(ms_done, n_ms[0])
                nc.gpsimd.tensor_tensor(rs, ms, expo[:, 0:ms.shape[1]], ALU.pow).then_inc(done, 1)

            def pre(n):
                pool.wait_ge(ssx_done, n + 1)
                inverse_rms(ssx[:, n:n + 1], msx[:, n:n + 1], rsx[:, n:n + 1], rsx_done, 1.0 / D)

            def of_att(h):
                pool.wait_ge(ssa_done, h + 1)
                inverse_rms(ssa[:, h:h + 1], msa[:, h:h + 1], rsa[:, h:h + 1], rsa_done, 1.0 / W_MOBA)

            def post(m, scale):
                pool.wait_ge(ssy_done, m + 1)
                inverse_rms(ssy[:, m:m + 1], msy[:, m:m + 1], rsy[:, m:m + 1], rsy_done, scale)

            for t in range(NT):
                pre(t)

            with nc.allow_non_contiguous_dma(reason="64 x 32 bias values"):
                for g in range(2):
                    pool.dma_start(relT[:, g, :], rel_bias[:, 8 * g:8 * g + 8].rearrange("b h -> h b")) \
                        .then_inc(small_loaded, 16)
            pool.dma_start(sinks[:, :], swa_sinks.to_broadcast([P, 8])).then_inc(small_loaded, 16)
            gain(g_b, ffn1_post_g, gain_b)
            gain(g_c, mix_pre_g, gain_c)
            gain(g_d, ffn2_post_g, gain_d)

            pool.wait_ge(small_loaded, 48)
            nc.gpsimd.tensor_scalar(nsink[:, :], sinks[:, :], -1.0, None, ALU.mult).then_inc(nsink_ready, 1)
            for b, (first, end) in enumerate(bucket_ranges()):
                nc.gpsimd.tensor_copy(rows[:, :, T - end:T - first],
                                      relT[:, :, b:b + 1].to_broadcast([8, 2, end - first])).then_inc(rows_ready, 1)
            nc.gpsimd.memset(rows[:, :, T:TAB], NEG).then_inc(rows_ready, 1)
            pool.wait_ge(rows_ready, BUCKETS + 1)
            nc.gpsimd.memset(rows[:, 1, 0:T - WINDOW], NEG).then_inc(rows_ready, 1)
            pool.wait_ge(rows_ready, BUCKETS + 2)
            for g in range(2):
                dst = scratch.rearrange("(q g h j) -> h g q j", g=3, h=8, j=TAB)[:, g]
                pool.dma_start(dst, rows[:, g:g + 1, :].to_broadcast([8, P, TAB])).then_inc(rows_stored, 16)

            pool.wait_ge(xn_ready, 4)
            gain(g_a, moba_out_g, gain_a, 0, W_MOBA)
            gain(g_a, swa_out_g, gain_a, W_MOBA, W_SWA)
            for t in range(NT):
                post(t, 4.0 / D)
                pre(4 + t)
            pool.wait_ge(branch_done, 4)
            gain(g_b, mix_post_g, gain_b)
            pool.wait_ge(xn_ready, 8)
            gain(g_c, ffn2_pre_g, gain_c)

            pool.wait_ge(rows_stored, 32)
            pool.wait_ge(nsink_ready, 1)

            def step_operands(i, first):
                if not first:
                    pool.wait_ge(logits_done, 16 * i - 8)
                    pool.wait_ge(exp_done, 16 * i - 8)
                pool.dma_start(bias_s[:, :, :], two_rows(i * TAB + 8 * TAB + T - 2 * P, 4 * TAB, 2 * P)) \
                    .then_inc(bias_s_loaded, 16)
                nc.gpsimd.tensor_copy(nsink_now[:, :], nsink[:, :].rearrange("p (e h) -> p h e", e=2)[:, bass.ds(i, 1), :]
                                      .rearrange("p a e -> p (a e)")).then_inc(sink_ready, 1)
                for parity in range(2):
                    nc.gpsimd.tensor_copy(s_win[:, :, parity, 2 * P:2 * P + 1],
                                          nsink[:, :].rearrange("p (e h) -> p e h", e=2)[:, :, bass.ds(i, 1)]) \
                        .then_inc(sink_ready, 1)
                if not first:
                    pool.wait_ge(logits_done, 16 * i)
                pool.dma_start(bias_m[:, :, :], two_rows(i * (2 * TAB), TAB, T)).then_inc(bias_m_loaded, 16)

            def two_rows(offset, pitch, n):
                return skewed[:, bass.ds(offset, 2 * pitch)].rearrange("q (e r) -> q e r", e=2)[:, :, 0:n]

            step_operands(0, True)
            with pool.Fori(1, PAIRS) as i:
                step_operands(i, False)

            for h in range(2 * NT):
                of_att(h)
            for t in range(NT):
                post(4 + t, 1.0 / D)
                pre(8 + t)
            for t in range(NT):
                post(8 + t, 4.0 / D)

        @block.tensor
        def _(pe):
            def three_passes(dst, a, b, start, stop):
                nc.tensor.matmul(dst, a[0], b[0], start=start, stop=False)
                nc.tensor.matmul(dst, a[0], b[1], start=False, stop=False)
                return nc.tensor.matmul(dst, a[1], b[0], start=False, stop=stop)

            def columns_product(c, bank, ks=range(KD), tokens=slice(0, T)):
                w = stationary_weights(c)
                for k in ks:
                    last = three_passes(ps[:, bank, tokens], [v[:, k, :] for v in w],
                                        [xT_hi[:, k, tokens], xT_lo[:, k, tokens]], k == 0, k == KD - 1)
                return last

            def first_panels(c, banks, n):
                for half in range(2):
                    pe.wait_ge(xT_hi_ready, 2 * (n + 2 * half + 2))
                    pe.wait_ge(xT_lo_ready, 2 * (n + 2 * half + 2))
                    for j in range(RING):
                        if half == 0:
                            wait_split(pe, c + j)
                        last = columns_product(c + j, banks[j], tokens=slice(T // 2 * half, T // 2 * (half + 1)))
                        if half == 1:
                            last.then_inc(panel_used, 1)
                        elif j in (0, 2):
                            transposes(n + 2 + j // 2)

            def up_tile(base, i, t):
                before = 0 if base == UP1 else NF
                pe.wait_ge(h_done, before + 2 * i + t - 1)
                for side in range(2):
                    wait_split(pe, base + 2 * t + side, i)
                    columns_product(base + 2 * t + side, 2 * side + t).then_inc(panel_used, 1)

            def up(base, n):
                first_panels(base, (0, 2, 1, 3), n)
                with pe.Fori(1, NF // 2) as i:
                    for t in range(2):
                        up_tile(base, i, t)

            def row_products(c, act_hi, act_lo, tok, start, stop, halves=(0, 1)):
                lhs = [act_hi[:, tok * P:(tok + 1) * P], act_lo[:, tok * P:(tok + 1) * P]]
                for half in halves:
                    cols = slice(512 * half, 512 * half + 512)
                    last = three_passes(ps[:, 2 * tok + half, :], lhs,
                                        [w_hi[:, c % RING, cols], w_lo[:, c % RING, cols]], start, stop)
                return last

            def down_panel(base, d, i=0, start=False):
                c = base + d
                wait_split(pe, c, i)
                n = (0 if base == DOWN1 else NF) + d + 4 * i + 1
                pe.wait_ge(hs_hi_ready, n)
                pe.wait_ge(hs_lo_ready, n)
                for tok in (2, 3, 0, 1):
                    if start and tok == 0:
                        pe.wait_ge(h_done, NF if base == DOWN1 else 2 * NF)
                    last = row_products(c, hs_hi[:, d % RING, :], hs_lo[:, d % RING, :], tok, start, False)
                last.then_inc(panel_used, 1)

            def transposes(n):
                tok = n % NT
                pe.wait_ge(xn_ready, n + 1)
                for k in range(KD):
                    last = nc.tensor.transpose(ps[:, 2 * tok + k // 4, k % 4 * P:(k % 4 + 1) * P],
                                               xn[:, n % 2, k * P:(k + 1) * P], ident[:, :])
                last.then_inc(xT_in_psum, 1)

            def last_rows(c0, acts, chain, staged=None):
                for tok in range(NT):
                    for j in range(RING):
                        if tok == 0:
                            wait_split(pe, c0 + j)
                            if staged is not None:
                                pe.wait_ge(hs_hi_ready, staged + j + 1)
                                pe.wait_ge(hs_lo_ready, staged + j + 1)
                        a_hi, a_lo = acts(j)
                        last = row_products(c0 + j, a_hi, a_lo, tok, False, j == RING - 1)
                        if tok == NT - 1:
                            last.then_inc(panel_used, 1)
                        elif j == RING - 1:
                            last.then_inc(y_done, 1)
                        if chain is not None and tok >= 2 and j == 1:
                            transposes(chain + tok - 2)

            def down(base, chain):
                for d in range(2):
                    down_panel(base, d, start=d == 0)
                with pe.Fori(0, (NF - 2) // RING - 1) as i:
                    for j in range(RING):
                        down_panel(base, 2 + j, i)
                d0 = NF - RING
                last_rows(base + d0, lambda j: (hs_hi[:, (d0 + j) % RING, :], hs_lo[:, (d0 + j) % RING, :]), chain,
                          (0 if base == DOWN1 else NF) + d0)

            pe.wait_ge(ident_ready, 1)
            for t in range(2):
                transposes(t)
            up(UP1, 0)
            down(DOWN1, 4)

            def values_to_tokens():
                for tok in range(NT):
                    last = nc.tensor.transpose(ps[:, 1, tok * P:(tok + 1) * P], vT[:, tok * P:(tok + 1) * P], ident[:, :])
                last.then_inc(turned_values, 1)

            def project(i, k, following):
                j = k // 4
                if k == 9:
                    pe.wait_ge(vT_ready, i + 2)
                    values_to_tokens()
                if j >= (4 if following else 2):
                    return
                if k == 0:
                    wait_split(pe, IN + 4, i)
                if k == 4:
                    pe.wait_ge(qm_ready, i + 1)
                    wait_split(pe, IN + 5, i)
                if k == 8:
                    pe.wait_ge(km_ready, i + 1)
                    wait_split(pe, IN + 6, i)
                if k == 12:
                    pe.wait_ge(vm_ready, i + 1)
                    wait_split(pe, IN + 7, i)
                last = columns_product(IN + 4 + j, j % 2, [2 * (k % 4), 2 * (k % 4) + 1])
                if k % 4 == 3:
                    last.then_inc(panel_used, 1)

            def scores(i, k):
                win, e, qt, kts = unit(k)
                g = UNITS * i + k
                if k == 0:
                    pe.wait_ge(qs_ready, i + 1)
                if k == 1 and isinstance(i, int) and i == 0:
                    pe.wait_ge(qm_ready, 1)
                if k == 8:
                    pe.wait_ge(km_ready, i + 1)
                if k >= 2:
                    pe.wait_ge(logits_done, g - 1)
                elif not isinstance(i, int):
                    pe.wait_ge(logits_done, g - 1)
                elif g >= 2:
                    pe.wait_ge(logits_done, g - 1)
                q, kk = (qs, ksT) if win else (qm, km)
                rows_ = slice(HD * e, HD * e + HD)
                nc.tensor.matmul(ps[:, 2 + k % 2, 0:len(kts) * P], q[rows_, qt * P:(qt + 1) * P],
                                 kk[rows_, kts[0] * P:(kts[-1] + 1) * P], start=True, stop=True).then_inc(scores_done, 1)

            def turn(i, k, first):
                win, e, qt, kts = unit(k)
                g = UNITS * i + k
                pe.wait_ge(exp_done, g + 1)
                if k >= 2 or not first:
                    pe.wait_ge(pT_by_act if k % 2 == 0 else pT_by_dve, 8 * i + k // 2)
                for n in range(len(kts)):
                    last = nc.tensor.transpose(ps[:, 4 + k % 2, n * P:(n + 1) * P], prob[:, k % RING, n * P:(n + 1) * P],
                                               ident[:, :])
                last.then_inc(pT_in_psum, 1)

            def values(i, k, first):
                win, e, qt, kts = unit(k)
                pe.wait_ge(pT_by_act if k % 2 == 0 else pT_by_dve, 8 * i + k // 2 + 1)
                if qt == 0 and (k >= 8 or not first):
                    pe.wait_ge(att_done, 4 * i + k // 4 - 1)
                if k == 8:
                    pe.wait_ge(vm_ready, i + 1)
                v = vs if win else vm
                for n, kt in enumerate(kts):
                    last = nc.tensor.matmul(ps[:, 6 + k // 4 % 2, qt * HD:(qt + 1) * HD], pT[:, k % 2, n * P:(n + 1) * P],
                                            v[:, kt, HD * e:HD * e + HD], start=n == 0, stop=n == len(kts) - 1)
                last.then_inc(pv_done, 1)

            first_panels(IN, (0, 1, 2, 3), 4)
            pe.wait_ge(vT_ready, 1)
            values_to_tokens()
            pe.wait_ge(ks_ready, 1)
            pe.wait_ge(vs_ready, 1)

            def att_transposes(h):
                pe.wait_ge(an_ready, h + 1)
                if h == 0:
                    pe.wait_ge(vm_ready, PAIRS)
                elif h < NT:
                    pe.wait_ge(aT_lo_ready, h)
                elif h < NT + 2:
                    pe.wait_ge(att_done, 4 * PAIRS)
                else:
                    pe.wait_ge(aT_lo_ready, h - 1)
                for n in range(4):
                    last = nc.tensor.transpose(ps[:, att_bank(h), n * P:(n + 1) * P],
                                               xn[:, h % 4 // 2, (h % 2 * 4 + n) * P:(h % 2 * 4 + n + 1) * P], ident[:, :])
                last.then_inc(aT_in_psum, 1)

            def window_rows(d, tok, halves=(0, 1)):
                k = W_MOBA // P + d
                return row_products(OUT + d, xT_hi[:, k, :], xT_lo[:, k, :], tok, d == 0, False, halves)

            def window_output(k):
                if 14 <= k < 14 + NT:
                    att_transposes(k - 14)
                if k in (16, 17):
                    if k == 16:
                        pe.wait_ge(km_ready, PAIRS)
                        pe.wait_ge(aT_hi_ready, 1)
                        pe.wait_ge(aT_lo_ready, 1)
                    for d in (2 * (k - 16), 2 * (k - 16) + 1):
                        wait_split(pe, OUT + d)
                        window_rows(d, 0, (0,))

            def attention(i, first, following):
                for k in range(UNITS if following else UNITS + DRAIN):
                    if k < UNITS:
                        scores(i, k)
                    if has_lagging(k, 2, first):
                        turn(*lagging(i, k, 2), first)
                    if has_lagging(k, 3, first):
                        values(*lagging(i, k, 3), first)
                    if k < UNITS:
                        project(i, k, following)
                    if not following:
                        window_output(k)

            attention(0, True, True)
            with pe.Fori(1, PAIRS - 1) as i:
                attention(i, False, True)
            attention(PAIRS - 1, False, False)

            pe.wait_ge(aT_lo_ready, NT)
            for d in range(RING):
                window_rows(d, 0, (1,))
            for d in range(RING):
                for tok in (1, 2):
                    if d == 0 and tok == 1:
                        pe.wait_ge(logits_done, PAIRS * UNITS)
                    elif d == 0:
                        pe.wait_ge(pT_by_act, PAIRS * UNITS // 2)
                        pe.wait_ge(pT_by_dve, PAIRS * UNITS // 2)
                    window_rows(d, tok)
                if d >= 1:
                    att_transposes(NT + d - 1)
            att_transposes(2 * NT - 1)
            for d in range(RING):
                if d == 0:
                    pe.wait_ge(aT_lo_ready, 2 * NT)
                window_rows(d, 3).then_inc(panel_used, 1)
            last_rows(OUT + RING, lambda j: (xT_hi[:, j, :], xT_lo[:, j, :]), 8)
            up(UP2, 8)
            down(DOWN2, None)

        @block.scalar
        def _(act):
            def split_hi(c, i=0, first=False):
                wait_loaded(act, c, i)
                if not first:
                    act.wait_ge(panel_used, c + 4 * i - RING + 1)
                nc.scalar.activation(w_hi[:, c % RING, :], raw[:, c % RING, :], ACT.Copy).then_inc(hi_ready, 1)

            squares = []

            def square_sum(src, dst, done, count):
                if len(squares) >= 2:
                    act.wait_ge(*squares[-2])
                nc.scalar.activation(junk[:, len(squares) % 2, 0:src.shape[1]], src, ACT.Square, accum_out=dst) \
                    .then_inc(done, 1)
                squares.append((done, count))

            def sum_y(m):
                if m % NT < NT - 1:
                    act.wait_ge(y_done, (NT - 1) * (m // NT) + m % NT + 1)
                else:
                    act.wait_ge(panel_used, (DOWN1 + NF, OUT + D // P, DOWN2 + NF)[m // NT])
                square_sum(bank2(m % NT), ssy[:, m:m + 1], ssy_done, m + 1)

            def sum_x(n, y=None):
                if y is not None:
                    act.wait_ge(x_ready, y + 1)
                square_sum(xres[:, n % NT, :], ssx[:, n:n + 1], ssx_done, n + 1)

            def turned_hi(n):
                tok = n % NT
                act.wait_ge(xT_in_psum, n + 1)
                for b in range(2):
                    nc.scalar.activation(xT_hi[:, 4 * b:4 * b + 4, tok * P:(tok + 1) * P],
                                         ps[:, 2 * tok + b, :].rearrange("p (k t) -> p k t", t=P), ACT.Copy) \
                        .then_inc(xT_hi_ready, 1)

            def silu(base, i, t):
                n = (0 if base == UP1 else NF) + 2 * i + t
                act.wait_ge(panel_used, base + 4 * i + 2 * t + 1)
                if not isinstance(i, int) or base == UP2:
                    act.wait_ge(h_done, n - 1)
                nc.scalar.activation(tmp[:, 512 * t:512 * t + 512], ps[:, t, :], ACT.Silu).then_inc(silu_done, 1)

            def up(base, down_base):
                for t in range(2):
                    split_hi(base + RING + t)
                    silu(base, 0, t)
                for d in range(2):
                    stage_hidden(down_base, d)
                with act.Fori(1, NF // 2) as i:
                    for t in range(2):
                        for side in range(2):
                            split_hi(base + 2 * t + side + LEAD, i)
                        silu(base, i, t)

            def stage_hidden(base, d, i=0):
                if d >= RING or not isinstance(i, int):
                    act.wait_ge(panel_used, base + d + 4 * i - RING + 1)
                act.wait_ge(h_done, (0 if base == DOWN1 else NF) + d + 4 * i + 1)
                nc.scalar.activation(hs_hi[:, d % RING, :], hT[:, bass.ds(d + 4 * i, 1), :].rearrange("p a t -> p (a t)"),
                                     ACT.Copy).then_inc(hs_hi_ready, 1)

            def down(base, chain):
                for d in range(2):
                    split_hi(base + d + LEAD)
                    stage_hidden(base, d + LEAD)
                with act.Fori(0, (NF - 2) // RING - 1) as i:
                    for j in range(RING):
                        split_hi(base + 2 + j + LEAD, i)
                        stage_hidden(base, 2 + j + LEAD, i)
                for d in range(NF - RING, NF - LEAD):
                    split_hi(base + d + LEAD)
                    stage_hidden(base, d + LEAD)

            def norms(m, n, following):
                for t in range(2):
                    sum_y(m + t)
                    sum_x(n + t, m + t)
                turned_hi(n)
                sum_y(m + 2)
                split_hi(following)
                turned_hi(n + 1)
                split_hi(following + 1)
                sum_x(n + 2, m + 2)
                sum_y(m + 3)
                split_hi(following + 2)
                turned_hi(n + 2)
                sum_x(n + 3, m + 3)
                split_hi(following + 3)
                turned_hi(n + 3)

            for t in range(0, NT, 2):
                for u in (t, t + 1):
                    act.wait_ge(x_loaded[u], 16)
                    sum_x(u)
                if t == 2:
                    split_hi(2, first=True)
                    split_hi(3, first=True)
                    turned_hi(2)
                    turned_hi(3)
                else:
                    split_hi(0, first=True)
                    turned_hi(0)
                    turned_hi(1)
                    split_hi(1, first=True)
            up(UP1, DOWN1)
            down(DOWN1, 4)
            norms(0, 4, IN)

            def evacuate(dst, wait, count, ready, bank, scale=1.0):
                act.wait_ge(wait, count)
                nc.scalar.activation(dst, ps[:, bank, :], ACT.Copy, scale=scale).then_inc(ready, 1)

            def project(i, k, following):
                if k % 4 == 1:
                    split_hi(IN + 4 + LEAD + k // 4, i)
                if k == 4:
                    evacuate(km[:, :], panel_used, IN + 4 * i + 5, km_ready, 0)
                if k == 10:
                    evacuate(vm[:, :, :].rearrange("p t c -> p (t c)"), turned_values, i + 2, vm_ready, 1)
                if k == 12 and following:
                    evacuate(qs[:, :], panel_used, IN + 4 * i + 7, qs_ready, 0, SCALE)

            def exponent(i, k, first):
                win, e, qt, kts = unit(k)
                g = UNITS * i + k
                act.wait_ge(logits_done, g + 1)
                if k >= RING or not first:
                    act.wait_ge(pT_in_psum, g - RING + 1)
                if k % 4 == 0 and not first:
                    act.wait_ge(att_done, 4 * i + k // 4 - 3)
                if k == 0:
                    act.wait_ge(sink_ready, 3 * (i + 1))
                n = len(kts) * P
                src = s_win[:, e, k % 2, 2 * P - n:2 * P + 1] if win else s_moba[:, k % 2, 0:n]
                nc.scalar.activation(prob[:, k % RING, 0:n + win], src, ACT.Exp, scale=-1.0, bias=nmax[:, k:k + 1],
                                     accum_out=psumrow[:, k:k + 1]).then_inc(exp_done, 1)

            def evacuate_turned(i, k, first):
                if k % 2:
                    return
                n = len(unit(k)[3]) * P
                act.wait_ge(pT_in_psum, UNITS * i + k + 1)
                if k >= 2 or not first:
                    act.wait_ge(pv_done, UNITS * i + k - 1)
                nc.scalar.activation(pT[:, 0, 0:n], ps[:, 4, 0:n], ACT.Copy).then_inc(pT_by_act, 1)

            evacuate(ksT[:, :], panel_used, IN + 1, ks_ready, 0)
            split_hi(IN + 4)
            split_hi(IN + 5)
            evacuate(vs[:, :, :].rearrange("p t c -> p (t c)"), turned_values, 1, vs_ready, 1)
            evacuate(qs[:, :], panel_used, IN + 3, qs_ready, 2, SCALE)

            def sum_att(h):
                square_sum(att[:, h % NT, att_cols(h)], ssa[:, h:h + 1], ssa_done, h + 1)

            def att_hi(h):
                tok, k0 = h % NT, att_cols(h).start // P
                act.wait_ge(aT_in_psum, h + 1)
                nc.scalar.activation(xT_hi[:, k0:k0 + 4, tok * P:(tok + 1) * P],
                                     ps[:, att_bank(h), :].rearrange("p (k t) -> p k t", t=P), ACT.Copy) \
                    .then_inc(aT_hi_ready, 1)

            def window_output(k):
                if 12 <= k < 12 + NT:
                    if k == 12:
                        act.wait_ge(att_done, 4 * PAIRS - 2)
                    sum_att(k - 12)
                if 15 <= k < 15 + NT:
                    att_hi(k - 15)

            def attention(i, first, following):
                for k in range(UNITS if following else UNITS + DRAIN):
                    if k < UNITS:
                        exponent(i, k, first)
                    if has_lagging(k, 2, first):
                        evacuate_turned(*lagging(i, k, 2), first)
                    if k < UNITS:
                        project(i, k, following)
                    if not following:
                        window_output(k)

            attention(0, True, True)
            with act.Fori(1, PAIRS - 1) as i:
                attention(i, False, True)
            attention(PAIRS - 1, False, False)

            act.wait_ge(att_done, 4 * PAIRS)
            for t in range(NT):
                sum_att(NT + t)
            for t in range(NT):
                att_hi(NT + t)
            for d in range(RING):
                split_hi(OUT + RING + d)
            norms(4, 8, UP2)
            up(UP2, DOWN2)
            down(DOWN2, None)
            for t in range(NT):
                sum_y(8 + t)

        @block.vector
        def _(dve):
            def split_lo(c, i=0):
                dve.wait_ge(hi_ready, c + 4 * i + 1)
                nc.vector.tensor_tensor(w_lo[:, c % RING, :], raw[:, c % RING, :], w_hi[:, c % RING, :].bitcast(F32),
                                        ALU.subtract).then_inc(lo_ready, 1)

            def branch(m, g):
                dve.wait_ge(rsy_done, m + 1)
                if m % NT:
                    dve.wait_ge(x_ready, m)
                nc.vector.scalar_tensor_tensor(out=tmp[:, :], in0=bank2(m % NT), scalar=rsy[:, m:m + 1], in1=g[:, :],
                                               op0=ALU.mult, op1=ALU.mult).then_inc(branch_done, 1)

            def residual(m):
                dve.wait_ge(branch_done, m + 1)
                nc.vector.tensor_tensor(xres[:, m % NT, :], xres[:, m % NT, :], tmp[:, :], ALU.add).then_inc(x_ready, 1)

            def normalise(n, g):
                dve.wait_ge(rsx_done, n + 1)
                if n >= 2:
                    dve.wait_ge(xT_in_psum, n - 1)
                nc.vector.scalar_tensor_tensor(out=xn[:, n % 2, :], in0=xres[:, n % NT, :], scalar=rsx[:, n:n + 1],
                                               in1=g[:, :], op0=ALU.mult, op1=ALU.mult).then_inc(xn_ready, 1)

            def turned_lo(n):
                tok = n % NT
                for b in range(2):
                    dve.wait_ge(xT_hi_ready, 2 * n + b + 1)
                    span = (slice(None), slice(4 * b, 4 * b + 4), slice(tok * P, (tok + 1) * P))
                    nc.vector.tensor_tensor(xT_lo[span], ps[:, 2 * tok + b, :].rearrange("p (k t) -> p k t", t=P),
                                            xT_hi[span].bitcast(F32), ALU.subtract).then_inc(xT_lo_ready, 1)

            def hidden(base, i, t):
                n = (0 if base == UP1 else NF) + 2 * i + t
                dve.wait_ge(silu_done, n + 1)
                dve.wait_ge(panel_used, base + 4 * i + 2 * t + 2)
                nc.vector.tensor_tensor(hT[:, bass.ds(2 * i + t, 1), :].rearrange("p a t -> p (a t)"),
                                        ps[:, 2 + t, :], tmp[:, 512 * t:512 * t + 512], ALU.mult).then_inc(h_done, 1)

            def up(base, down_base):
                for t in range(2):
                    split_lo(base + RING + t)
                    hidden(base, 0, t)
                for d in range(2):
                    stage_hidden(down_base, d)
                with dve.Fori(1, NF // 2) as i:
                    for t in range(2):
                        for side in range(2):
                            split_lo(base + 2 * t + side + LEAD, i)
                        hidden(base, i, t)

            def stage_hidden(base, d, i=0):
                dve.wait_ge(hs_hi_ready, (0 if base == DOWN1 else NF) + d + 4 * i + 1)
                nc.vector.tensor_tensor(hs_lo[:, d % RING, :], hT[:, bass.ds(d + 4 * i, 1), :].rearrange("p a t -> p (a t)"),
                                        hs_hi[:, d % RING, :].bitcast(F32), ALU.subtract).then_inc(hs_lo_ready, 1)

            def down(base):
                for d in range(2):
                    split_lo(base + d + LEAD)
                    stage_hidden(base, d + LEAD)
                with dve.Fori(0, (NF - 2) // RING - 1) as i:
                    for j in range(RING):
                        split_lo(base + 2 + j + LEAD, i)
                        stage_hidden(base, 2 + j + LEAD, i)
                for d in range(NF - RING, NF - LEAD):
                    split_lo(base + d + LEAD)
                    stage_hidden(base, d + LEAD)

            def norms(m, n, g_post, g_pre, following):
                for t in range(2):
                    branch(m + t, g_post)
                    residual(m + t)
                    normalise(n + t, g_pre)
                turned_lo(n)
                branch(m + 2, g_post)
                split_lo(following)
                residual(m + 2)
                turned_lo(n + 1)
                split_lo(following + 1)
                normalise(n + 2, g_pre)
                branch(m + 3, g_post)
                residual(m + 3)
                split_lo(following + 2)
                turned_lo(n + 2)
                normalise(n + 3, g_pre)
                split_lo(following + 3)
                turned_lo(n + 3)

            dve.wait_ge(gain_a, 16)
            for t in range(0, NT, 2):
                normalise(t, g_a)
                normalise(t + 1, g_a)
                if t == 2:
                    split_lo(2)
                    split_lo(3)
                    turned_lo(2)
                    turned_lo(3)
                else:
                    split_lo(0)
                    turned_lo(0)
                    turned_lo(1)
                    split_lo(1)
            up(UP1, DOWN1)
            down(DOWN1)
            dve.wait_ge(gain_b, 16)
            dve.wait_ge(gain_c, 16)
            norms(0, 4, g_b, g_c, IN)

            def evacuate(dst, count, ready, bank, scale=1.0):
                dve.wait_ge(panel_used, count)
                nc.vector.tensor_scalar(dst, ps[:, bank, :], scale, None, ALU.mult).then_inc(ready, 1)

            def project(i, k, following):
                if k % 4 == 1:
                    split_lo(IN + 4 + LEAD + k // 4, i)
                if k == 8:
                    evacuate(vT[:, :], IN + 4 * i + 6, vT_ready, 1)

            def queries(i):
                evacuate(qm[:, :], IN + 4 * i + 4, qm_ready, 1, SCALE)

            def logits(i, k, first):
                win, e, qt, kts = unit(k)
                g = UNITS * i + k
                dve.wait_ge(scores_done, g + 1)
                if k >= 2 or not first:
                    dve.wait_ge(exp_done, g - 1)
                n = len(kts) * P
                if k == 0:
                    dve.wait_ge(bias_s_loaded, 16 * (i + 1))
                    dve.wait_ge(sink_ready, 3 * (i + 1))
                if k == 8:
                    dve.wait_ge(bias_m_loaded, 16 * (i + 1))
                if not isinstance(i, int):
                    hold_here(dve, dve_held)
                nc.vector.tensor_tensor_reduce(
                    out=s_win[:, e, k % 2, 2 * P - n:2 * P] if win else s_moba[:, k % 2, 0:n],
                    in0=ps[:, 2 + k % 2, 0:n], in1=bias_s[:, e, 2 * P - n:2 * P] if win else bias_m[:, e, T - n:T],
                    scale=-1.0, scalar=nsink_now[:, e:e + 1] if win else BIG, op0=ALU.add, op1=ALU.min,
                    accum_out=nmax[:, k:k + 1]).then_inc(logits_done, 1)

            def evacuate_turned(i, k, first):
                if k % 2 == 0:
                    return
                n = len(unit(k)[3]) * P
                dve.wait_ge(pT_in_psum, UNITS * i + k + 1)
                if k >= 2 or not first:
                    dve.wait_ge(pv_done, UNITS * i + k - 1)
                nc.vector.tensor_copy(pT[:, 1, 0:n], ps[:, 5, 0:n]).then_inc(pT_by_dve, 1)

            def head_done(i, h):
                g = 4 * i + h
                win, e = h < 2, h % 2
                dve.wait_ge(pv_done, 4 * (g + 1))
                dve.wait_ge(exp_done, 4 * (g + 1))
                nc.vector.reciprocal(rinv[:, 4 * h:4 * h + 4], psumrow[:, 4 * h:4 * h + 4]).then_inc(rinv_done, 1)
                dve.wait_ge(rinv_done, g + 1)
                col = W_MOBA + (i + 4 * e) * HD if win else (2 * i + e) * HD
                nc.vector.tensor_tensor(att[:, :, bass.ds(col, HD)],
                                        ps[:, 6 + e, 0:4 * HD].rearrange("p (t c) -> p t c", c=HD),
                                        rinv[:, 4 * h:4 * h + 4].rearrange("p (t a) -> p t a", a=1)
                                        .to_broadcast([P, NT, HD]), ALU.mult).then_inc(att_done, 1)

            evacuate(vT[:, :], IN + 2, vT_ready, 1)
            evacuate(qm[:, :], IN + 4, qm_ready, 3, SCALE)
            split_lo(IN + 4)
            split_lo(IN + 5)

            def normalise_att(h):
                dve.wait_ge(rsa_done, h + 1)
                if h >= NT:
                    dve.wait_ge(aT_in_psum, h - NT + 1)
                cols = att_cols(h)
                nc.vector.scalar_tensor_tensor(out=xn[:, h % 4 // 2, h % 2 * 512:(h % 2 + 1) * 512],
                                               in0=att[:, h % NT, cols], scalar=rsa[:, h:h + 1], in1=g_a[:, cols],
                                               op0=ALU.mult, op1=ALU.mult).then_inc(an_ready, 1)

            def att_lo(h):
                tok, k0 = h % NT, att_cols(h).start // P
                dve.wait_ge(aT_hi_ready, h + 1)
                span = (slice(None), slice(k0, k0 + 4), slice(tok * P, (tok + 1) * P))
                nc.vector.tensor_tensor(xT_lo[span], ps[:, att_bank(h), :].rearrange("p (k t) -> p k t", t=P),
                                        xT_hi[span].bitcast(F32), ALU.subtract).then_inc(aT_lo_ready, 1)

            def window_output(k):
                if 13 <= k < 13 + NT:
                    if k == 13:
                        dve.wait_ge(gain_a, 48)
                    normalise_att(k - 13)
                if 15 <= k < 15 + NT:
                    att_lo(k - 15)

            def attention(i, first, following):
                for k in range(UNITS if following else UNITS + DRAIN):
                    if k < UNITS:
                        logits(i, k, first)
                    if has_lagging(k, 2, first):
                        evacuate_turned(*lagging(i, k, 2), first)
                    if k % 4 == 3 and k >= 7 and k < UNITS:
                        head_done(i, k // 4 - 1)
                    if k == 3 and not first:
                        head_done(i - 1, 3)
                    if k == 1 and not first:
                        queries(i)
                    if k < UNITS:
                        project(i, k, following)
                    if not following and k < UNITS + DRAIN - 1:
                        window_output(k)
                if not following:
                    head_done(i, 3)

            attention(0, True, True)
            with dve.Fori(1, PAIRS - 1) as i:
                attention(i, False, True)
            attention(PAIRS - 1, False, False)

            att_lo(NT - 1)
            for t in range(NT):
                normalise_att(NT + t)
                if t >= 1:
                    att_lo(NT + t - 1)
            att_lo(2 * NT - 1)
            for d in range(RING):
                split_lo(OUT + RING + d)
            dve.wait_ge(gain_b, 32)
            dve.wait_ge(gain_c, 32)
            norms(4, 8, g_b, g_c, UP2)
            up(UP2, DOWN2)
            down(DOWN2)
            dve.wait_ge(gain_d, 16)
            for t in range(NT):
                branch(8 + t, g_d)
                residual(8 + t)


_INS = ['x', 'ffn1_pre_g', 'ffn1_w_gate', 'ffn1_w_up', 'ffn1_w_down', 'ffn1_post_g', 'mix_pre_g', 'w_in', 'rel_bias',
        'moba_out_g', 'swa_sinks', 'swa_out_g', 'w_out', 'mix_post_g', 'ffn2_pre_g', 'ffn2_w_gate', 'ffn2_w_up',
        'ffn2_w_down', 'ffn2_post_g']
_OUTS = [((1, T, D), 'float32')]


def kernel(**inputs):
    import numpy as _np
    import concourse.bacc as _bacc
    from concourse import mybir as _mybir
    from concourse.bass_utils import run_bass_kernel_spmd as _run

    nc = _bacc.Bacc("TRN2", target_bir_lowering=False, num_devices=1)
    arrays, args = {}, []
    for name in _INS:
        a = _np.ascontiguousarray(inputs[name])
        arrays[f"in_{name}_dram"] = a
        args.append(nc.dram_tensor(f"in_{name}_dram", a.shape, _mybir.dt.from_np(a.dtype), kind="ExternalInput").ap())
    for i, (shape, dtype) in enumerate(_OUTS):
        dt = _mybir.dt.from_np(_np.dtype(dtype))
        args.append(nc.dram_tensor(f"out_{i}_dram", shape, dt, kind="ExternalOutput").ap())
    build(nc, *args)
    r = _run(nc, [arrays], core_ids=[0])
    got = tuple(r.results[0][f"out_{i}_dram"] for i in range(len(_OUTS)))
    return got[0]
```

```python
import math
from contextlib import ExitStack

import numpy as np
import concourse.bass as bass
from concourse import mybir

ALU = mybir.AluOpType
ACT = mybir.ActivationFunctionType
F32 = mybir.dt.float32
F32R = mybir.dt.float32r
BF16 = mybir.dt.bfloat16

P = 128
D = 1024
T = 512
F = 2816
KD = D // P
NT = T // P
NF = F // P
HD = 64
W_MOBA = 512
W_SWA = 512
BUCKETS = 32
MAX_DISTANCE = 128
WINDOW = 128
EPS = 1e-6
NEG = -1e30
BIG = 3.0e38
SCALE = HD ** -0.5

RING = 4
UP1 = 0
DOWN1 = UP1 + 2 * NF
IN = DOWN1 + NF
OUT = IN + 18
UP2 = OUT + D // P
DOWN2 = UP2 + 2 * NF
PANELS = DOWN2 + NF
LEAD = 2

PAIRS = 4
UNITS = 16
DRAIN = 3
AT_SQUARE, AT_NORMALISE, AT_TURN, AT_SPLIT = (11, 12, 13, 14), (12, 14, 15, 16), (14, 16, 17, 18), (14, 17, 18, 19)
SPLIT_AT = (1, 5, 9, 13)
LAST_SPLIT_AT = (1, 3, 4, 15)
WARM_UP = 30
TAB = 640


def bucket_ranges():
    exact = BUCKETS // 2

    def bucket(n):
        if n < exact:
            return n
        large = exact + int(np.float32(np.log(np.float32(n) / np.float32(exact)) / np.float32(math.log(MAX_DISTANCE / exact)))
                            * np.float32(BUCKETS - exact))
        return min(large, BUCKETS - 1)

    of = [bucket(n) for n in range(T)]
    return [(of.index(b), T - of[::-1].index(b)) for b in range(BUCKETS)]


def build(nc, x, ffn1_pre_g, ffn1_w_gate, ffn1_w_up, ffn1_w_down, ffn1_post_g, mix_pre_g, w_in, rel_bias,
          moba_out_g, swa_sinks, swa_out_g, w_out, mix_post_g, ffn2_pre_g, ffn2_w_gate, ffn2_w_up,
          ffn2_w_down, ffn2_post_g, out):
    ctx = ExitStack()
    with ctx:
        def sb(name, shape, dt=F32, scope=ctx):
            return scope.enter_context(nc.sbuf_tensor(name, shape, dt))

        def sem(name):
            return ctx.enter_context(nc.semaphore(name))

        ps = ctx.enter_context(nc.psum_tensor("ps", [P, 8, 512], F32))
        xres = sb("xres", [P, NT, D])
        xT_hi = sb("xT_hi", [P, KD, T], F32R)
        xT_lo = sb("xT_lo", [P, KD, T], F32R)
        raw = sb("raw", [P, RING, 1024])
        w_hi = sb("w_hi", [P, RING, 1024], F32R)
        w_lo = sb("w_lo", [P, RING, 1024], F32R)
        g_a = sb("g_a", [P, D])
        g_b = sb("g_b", [P, D])
        g_c = sb("g_c", [P, D])
        g_d = sb("g_d", [P, D])
        xn = sb("xn", [P, 2, D])
        tmp = sb("tmp", [P, D])
        junk = sb("junk", [P, 2, D], BF16)
        ident = sb("ident", [P, P])
        expo = sb("expo", [P, 2])
        ssy = sb("ssy", [P, 12])
        msy = sb("msy", [P, 12])
        rsy = sb("rsy", [P, 12])
        ssx = sb("ssx", [P, 12])
        msx = sb("msx", [P, 12])
        rsx = sb("rsx", [P, 12])
        ssa = sb("ssa", [P, 2 * NT])
        msa = sb("msa", [P, 2 * NT])
        rsa = sb("rsa", [P, 2 * NT])
        sinks = sb("sinks", [P, 8])
        nsink = sb("nsink", [P, 8])
        relT = sb("relT", [8, 2, BUCKETS])
        rows = sb("rows", [8, 2, TAB])
        with ExitStack() as only_ffn:
            hT = sb("hT", [P, NF, T], F32, only_ffn)
            hs_hi = sb("hs_hi", [P, RING, T], F32R, only_ffn)
            hs_lo = sb("hs_lo", [P, RING, T], F32R, only_ffn)
        qs, qm = sb("qs", [P, 2, T], F32R), sb("qm", [P, 2, T], F32R)
        ks_hi, km_hi = sb("ks_hi", [P, 2, T], F32R), sb("km_hi", [P, 2, T], F32R)
        ks_lo, km_lo = sb("ks_lo", [P, T], F32R), sb("km_lo", [P, T], F32R)
        vs = sb("vs", [P, NT, P])
        vT = sb("vT", [P, T])
        vm = sb("vm", [P, NT, P])
        bias_s = sb("bias_s", [P, 2, 2 * P])
        bias_m = sb("bias_m", [P, 2, T])
        nsink_now = sb("nsink_now", [P, 2])
        s_win = sb("s_win", [P, 2, 2, 2 * P + 1])
        s_moba = sb("s_moba", [P, 2, T])
        prob = sb("prob", [P, RING, T + 2])
        pT = sb("pT", [P, 2, T])
        nmax = sb("nmax", [P, UNITS])
        psumrow = sb("psumrow", [P, UNITS])
        rinv = sb("rinv", [P, UNITS])
        att = sb("att", [P, NT, D])

        PITCH = 24 * TAB
        scratch = nc.dram_tensor("bias_rows", (P * PITCH,), F32, kind="Internal").ap()
        skewed = scratch[P - 1:P - 1 + P * (PITCH - 1)].rearrange("(q r) -> q r", r=PITCH - 1)

        x_loaded = [sem(f"x_loaded{t}") for t in range(NT)]
        gain_a, gain_b, gain_c, gain_d = sem("gain_a"), sem("gain_b"), sem("gain_c"), sem("gain_d")
        small_loaded = sem("small_loaded")
        raw_loaded = [sem(f"raw_loaded{s}") for s in range(RING)]
        hi_ready, lo_ready, panel_used = sem("hi_ready"), sem("lo_ready"), sem("panel_used")
        silu_done, h_done = sem("silu_done"), sem("h_done")
        hs_hi_ready, hs_lo_ready = sem("hs_hi_ready"), sem("hs_lo_ready")
        y_done, ssy_done, rsy_done = sem("y_done"), sem("ssy_done"), sem("rsy_done")
        branch_done, x_ready = sem("branch_done"), sem("x_ready")
        ssx_done, rsx_done, xn_ready = sem("ssx_done"), sem("rsx_done"), sem("xn_ready")
        xT_in_psum, xT_hi_ready, xT_lo_ready = sem("xT_in_psum"), sem("xT_hi_ready"), sem("xT_lo_ready")
        const_ready, pool_step, ident_ready = sem("const_ready"), sem("pool_step"), sem("ident_ready")
        ms_done = sem("ms_done")
        rows_ready, rows_stored = sem("rows_ready"), sem("rows_stored")
        nsink_ready = sem("nsink_ready")
        ks_ready, vs_ready, vT_ready, turned_values = sem("ks_ready"), sem("vs_ready"), sem("vT_ready"), sem("turned_values")
        ks_hi_ready, km_hi_ready = sem("ks_hi_ready"), sem("km_hi_ready")
        qs_hi_ready, qm_hi_ready = sem("qs_hi_ready"), sem("qm_hi_ready")
        qs_ready, qm_ready, km_ready, vm_ready = sem("qs_ready"), sem("qm_ready"), sem("km_ready"), sem("vm_ready")
        bias_s_loaded, bias_m_loaded, sink_ready = sem("bias_s_loaded"), sem("bias_m_loaded"), sem("sink_ready")
        scores_done, logits_done, exp_done = sem("scores_done"), sem("logits_done"), sem("exp_done")
        pT_in_psum, pT_by_act, pT_by_dve = sem("pT_in_psum"), sem("pT_by_act"), sem("pT_by_dve")
        pv_done, rinv_done, att_done = sem("pv_done"), sem("rinv_done"), sem("att_done")
        ssa_done, rsa_done, an_ready = sem("ssa_done"), sem("rsa_done"), sem("an_ready")
        aT_in_psum, aT_hi_ready, aT_lo_ready = sem("aT_in_psum"), sem("aT_hi_ready"), sem("aT_lo_ready")
        out_stored = sem("out_stored")
        dve_held = sem("dve_held")

        def bank2(tok):
            return ps[:, 2 * tok:2 * tok + 2, :].rearrange("p b n -> p (b n)")

        def att_cols(h):
            return slice(W_MOBA, D) if h < NT else slice(0, W_MOBA)

        def att_bank(h):
            return 1 if h < NT else 6 + h % 2

        def unit(k):
            win, e, qt = k < 8, k // 4 % 2, k % 4
            return win, e, qt, list(range(max(qt - 1, 0), qt + 1)) if win else list(range(qt + 1))

        def lagging(i, k, lag):
            return (i, k - lag) if k >= lag else (i - 1, k - lag + UNITS)

        HALVES = (slice(0, HD), slice(HD, P))

        def has_lagging(k, lag, first):
            return k - lag < UNITS and (k >= lag or not first)

        def wait_loaded(eng, c, i=0):
            n = c // RING + i + 1
            if c % RING == 0 and c >= IN:
                n = n + (c // RING + i - IN // RING if c < UP2 else UP2 // RING - 1 - IN // RING)
            eng.wait_ge(raw_loaded[c % RING], 16 * n)

        def wait_split(eng, c, i=0):
            eng.wait_ge(hi_ready, c + 4 * i + 1)
            eng.wait_ge(lo_ready, c + 4 * i + 1)

        def stationary_weights(c):
            return [w[:, c % RING, :].rearrange("p (k f) -> p k f", f=P) for w in (w_hi, w_lo)]

        block = ctx.enter_context(nc.Block())

        def hold_here(eng, counter):
            eng.sem_inc(counter, 1)

        @block.sync
        def _(sp):
            def load_x(t):
                sp.dma_start(xres[:, t, :], x[0, t * P:(t + 1) * P, :]).then_inc(x_loaded[t], 16)

            def wait_free(c, i):
                sp.wait_ge(lo_ready, c + 4 * i - RING + 1)

            def column_panel(c, i, w, col, free=True):
                if free:
                    wait_free(c, i)
                sp.dma_start(raw[:, c % RING, :].rearrange("p (k f) -> p k f", f=P),
                             w[0, :, bass.ds(col, P)].rearrange("(k p) f -> p k f", p=P)) \
                    .then_inc(raw_loaded[c % RING], 16)

            def row_panel(c, i, w, row):
                wait_free(c, i)
                parts = 2 if c % RING == 0 and IN <= c < UP2 else 1
                for n in range(parts):
                    cols = slice(n * (D // parts), (n + 1) * (D // parts))
                    sp.dma_start(raw[:, c % RING, cols], w[0, bass.ds(row, P), cols]).then_inc(raw_loaded[c % RING], 16)

            def up_panels(base, w_gate, w_up):
                if base == 0:
                    for j in range(RING):
                        load_x(j)
                        if j % 2 == 0:
                            continue
                        for p in (j - 1, j):
                            column_panel(p, 0, (w_gate, w_up)[p % 2], p // 2 * P, free=False)
                with sp.Fori(1 if base == 0 else 0, NF // 2) as i:
                    for j in range(RING):
                        column_panel(base + j, i, (w_gate, w_up)[j % 2], (2 * i + j // 2) * P)

            def down_panels(base, w):
                for d in range(2):
                    row_panel(base + d, 0, w, d * P)
                with sp.Fori(0, (NF - 2) // RING) as i:
                    for j in range(RING):
                        row_panel(base + 2 + j, i, w, (2 + 4 * i + j) * P)

            up_panels(UP1, ffn1_w_gate, ffn1_w_up)
            down_panels(DOWN1, ffn1_w_down)
            window_q = 3 * W_MOBA
            window_kv = window_q + W_SWA
            for j in range(2):
                column_panel(IN + j, 0, w_in, window_kv + j * P)
            with sp.Fori(0, PAIRS) as i:
                c = IN + 2
                wait_free(c, i)
                for h in range(2):
                    sp.dma_start(raw[:, c % RING, :].rearrange("p (k f) -> p k f", f=P)[:, :, HD * h:HD * h + HD],
                                 w_in[0, :, bass.ds(window_q + (i + 4 * h) * HD, HD)]
                                 .rearrange("(k p) f -> p k f", p=P)).then_inc(raw_loaded[c % RING], 16)
                for j in range(3):
                    column_panel(c + 1 + j, i, w_in, j * W_MOBA + i * P)
            for d in range(D // P):
                row_panel(OUT + d, 0, w_out, (d + W_MOBA // P) * P % D)
            up_panels(UP2, ffn2_w_gate, ffn2_w_up)
            down_panels(DOWN2, ffn2_w_down)
            for t in range(NT - 1):
                sp.wait_ge(x_ready, 2 * NT + t + 1)
                sp.dma_start(out[0, t * P:(t + 1) * P, :], xres[:, t, :]).then_inc(out_stored, 16)
            for half in range(2):
                cols = slice(D // 2 * half, D // 2 * (half + 1))
                sp.wait_ge(x_ready, 3 * NT + half)
                sp.dma_start(out[0, (NT - 1) * P:, cols], xres[:, NT - 1, cols]).then_inc(out_stored, 16)
            sp.wait_ge(out_stored, 16 * (NT + 1))

        @block.gpsimd
        def _(pool):
            def gain(dst, src, done, c0=0, n=D):
                pool.dma_start(dst[:, c0:c0 + n], src.to_broadcast([P, n])).then_inc(done, 16)

            gain(g_a, ffn1_pre_g, gain_a)
            nc.gpsimd.memset(expo[:, :], -0.5).then_inc(const_ready, 1)
            nc.gpsimd.memset(ident[:, :], 0.0).then_inc(const_ready, 1)
            pool.wait_ge(const_ready, 2)
            nc.gpsimd.affine_select(out=ident[:, :], in_=ident[:, :], compare_op=ALU.not_equal, fill=1.0, base=0,
                                    pattern=[[-1, P]], channel_multiplier=1).then_inc(ident_ready, 1)

            n_ms = [0]

            def inverse_rms(ss, ms, rs, done, scale):
                eps = EPS * (4 if scale == 4.0 / D else 1)
                nc.gpsimd.tensor_scalar(ms, ss, scale, eps, ALU.mult, ALU.add).then_inc(ms_done, 1)
                n_ms[0] += 1
                pool.wait_ge(ms_done, n_ms[0])
                nc.gpsimd.tensor_tensor(rs, ms, expo[:, 0:ms.shape[1]], ALU.pow).then_inc(done, 1)

            def pre(n):
                pool.wait_ge(ssx_done, n + 1)
                inverse_rms(ssx[:, n:n + 1], msx[:, n:n + 1], rsx[:, n:n + 1], rsx_done, 1.0 / D)

            def of_att(h):
                pool.wait_ge(ssa_done, h + 1)
                inverse_rms(ssa[:, h:h + 1], msa[:, h:h + 1], rsa[:, h:h + 1], rsa_done, 1.0 / W_MOBA)

            def post(m, scale):
                pool.wait_ge(ssy_done, m + 1)
                inverse_rms(ssy[:, m:m + 1], msy[:, m:m + 1], rsy[:, m:m + 1], rsy_done, scale)

            for t in range(NT):
                pre(t)

            with nc.allow_non_contiguous_dma(reason="64 x 32 bias values"):
                for g in range(2):
                    pool.dma_start(relT[:, g, :], rel_bias[:, 8 * g:8 * g + 8].rearrange("b h -> h b")) \
                        .then_inc(small_loaded, 16)
            pool.dma_start(sinks[:, :], swa_sinks.to_broadcast([P, 8])).then_inc(small_loaded, 16)
            gain(g_b, ffn1_post_g, gain_b)
            gain(g_c, mix_pre_g, gain_c)
            gain(g_d, ffn2_post_g, gain_d)

            pool.wait_ge(small_loaded, 48)
            nc.gpsimd.tensor_scalar(nsink[:, :], sinks[:, :], -1.0, None, ALU.mult).then_inc(nsink_ready, 1)
            for b, (first, end) in enumerate(bucket_ranges()):
                nc.gpsimd.tensor_copy(rows[:, :, T - end:T - first],
                                      relT[:, :, b:b + 1].to_broadcast([8, 2, end - first])).then_inc(rows_ready, 1)
            nc.gpsimd.memset(rows[:, :, T:TAB], NEG).then_inc(rows_ready, 1)
            pool.wait_ge(rows_ready, BUCKETS + 1)
            nc.gpsimd.memset(rows[:, 1, 0:T - WINDOW], NEG).then_inc(rows_ready, 1)
            pool.wait_ge(rows_ready, BUCKETS + 2)
            for g in range(2):
                dst = scratch.rearrange("(q g h j) -> h g q j", g=3, h=8, j=TAB)[:, g]
                pool.dma_start(dst, rows[:, g:g + 1, :].to_broadcast([8, P, TAB])).then_inc(rows_stored, 16)

            pool.wait_ge(xn_ready, 4)
            gain(g_a, moba_out_g, gain_a, 0, W_MOBA)
            gain(g_a, swa_out_g, gain_a, W_MOBA, W_SWA)
            for t in range(NT):
                post(t, 4.0 / D)
                pre(4 + t)
            pool.wait_ge(branch_done, 4)
            gain(g_b, mix_post_g, gain_b)
            pool.wait_ge(xn_ready, 8)
            gain(g_c, ffn2_pre_g, gain_c)

            pool.wait_ge(rows_stored, 32)
            pool.wait_ge(nsink_ready, 1)

            def step_operands(i, first):
                if not first:
                    pool.wait_ge(logits_done, 16 * i - 8)
                    pool.wait_ge(exp_done, 16 * i - 8)
                pool.dma_start(bias_s[:, :, :], two_rows(i * TAB + 8 * TAB + T - 2 * P, 4 * TAB, 2 * P)) \
                    .then_inc(bias_s_loaded, 16)
                nc.gpsimd.tensor_copy(nsink_now[:, :], nsink[:, :].rearrange("p (e h) -> p h e", e=2)[:, bass.ds(i, 1), :]
                                      .rearrange("p a e -> p (a e)")).then_inc(sink_ready, 1)
                for parity in range(2):
                    nc.gpsimd.tensor_copy(s_win[:, :, parity, 2 * P:2 * P + 1],
                                          nsink[:, :].rearrange("p (e h) -> p e h", e=2)[:, :, bass.ds(i, 1)]) \
                        .then_inc(sink_ready, 1)
                if not first:
                    pool.wait_ge(logits_done, 16 * i)
                pool.dma_start(bias_m[:, :, :], two_rows(i * (2 * TAB), TAB, T)).then_inc(bias_m_loaded, 16)

            def two_rows(offset, pitch, n):
                return skewed[:, bass.ds(offset, 2 * pitch)].rearrange("q (e r) -> q e r", e=2)[:, :, 0:n]

            step_operands(0, True)
            with pool.Fori(1, PAIRS) as i:
                step_operands(i, False)

            for h in range(2 * NT):
                of_att(h)
            for t in range(NT):
                post(4 + t, 1.0 / D)
                pre(8 + t)
            for t in range(NT):
                post(8 + t, 4.0 / D)

        @block.tensor
        def _(pe):
            def three_passes(dst, a, b, start, stop):
                nc.tensor.matmul(dst, a[0], b[0], start=start, stop=False)
                nc.tensor.matmul(dst, a[0], b[1], start=False, stop=False)
                return nc.tensor.matmul(dst, a[1], b[0], start=False, stop=stop)

            def columns_product(c, bank, ks=range(KD), tokens=slice(0, T)):
                w = stationary_weights(c)
                for k in ks:
                    last = three_passes(ps[:, bank, tokens], [v[:, k, :] for v in w],
                                        [xT_hi[:, k, tokens], xT_lo[:, k, tokens]], k == 0, k == KD - 1)
                return last

            def first_panels(c, banks, n):
                for half in range(2):
                    tokens = slice(T // 2 * half, T // 2 * (half + 1))
                    for j in range(RING):
                        if half == 0:
                            wait_split(pe, c + j)
                        for quarter in range(2):
                            if j == 0:
                                pe.wait_ge(xT_hi_ready, 2 * (n + 2 * half + 1) + quarter + 1)
                                pe.wait_ge(xT_lo_ready, 2 * (n + 2 * half + 1) + quarter + 1)
                            last = columns_product(c + j, banks[j], range(4 * quarter, 4 * quarter + 4), tokens)
                        if half == 1:
                            last.then_inc(panel_used, 1)
                        elif j in (0, 2):
                            transposes(n + 2 + j // 2)

            def up_tile(base, i, t):
                before = 0 if base == UP1 else NF
                pe.wait_ge(h_done, before + 2 * i + t - 1)
                for side in range(2):
                    wait_split(pe, base + 2 * t + side, i)
                    columns_product(base + 2 * t + side, 2 * side + t).then_inc(panel_used, 1)

            def up(base, n):
                first_panels(base, (0, 2, 1, 3), n)
                with pe.Fori(1, NF // 2) as i:
                    for t in range(2):
                        up_tile(base, i, t)

            def row_products(c, act_hi, act_lo, tok, start, stop, halves=(0, 1)):
                lhs = [act_hi[:, tok * P:(tok + 1) * P], act_lo[:, tok * P:(tok + 1) * P]]
                for half in halves:
                    cols = slice(512 * half, 512 * half + 512)
                    last = three_passes(ps[:, 2 * tok + half, :], lhs,
                                        [w_hi[:, c % RING, cols], w_lo[:, c % RING, cols]], start, stop)
                return last

            def down_panel(base, d, i=0, start=False):
                c = base + d
                wait_split(pe, c, i)
                n = (0 if base == DOWN1 else NF) + d + 4 * i + 1
                pe.wait_ge(hs_hi_ready, n)
                pe.wait_ge(hs_lo_ready, n)
                for tok in (2, 3, 0, 1):
                    if start and tok == 0:
                        pe.wait_ge(h_done, NF if base == DOWN1 else 2 * NF)
                    last = row_products(c, hs_hi[:, d % RING, :], hs_lo[:, d % RING, :], tok, start, False)
                last.then_inc(panel_used, 1)

            def transposes(n):
                tok = n % NT
                pe.wait_ge(xn_ready, n + 1)
                for k in range(KD):
                    last = nc.tensor.transpose(ps[:, 2 * tok + k // 4, k % 4 * P:(k % 4 + 1) * P],
                                               xn[:, n % 2, k * P:(k + 1) * P], ident[:, :])
                last.then_inc(xT_in_psum, 1)

            def last_rows(c0, acts, chain, staged=None):
                for tok in range(NT):
                    for j in range(RING):
                        if tok == 0:
                            wait_split(pe, c0 + j)
                            if staged is not None:
                                pe.wait_ge(hs_hi_ready, staged + j + 1)
                                pe.wait_ge(hs_lo_ready, staged + j + 1)
                        a_hi, a_lo = acts(j)
                        last = row_products(c0 + j, a_hi, a_lo, tok, False, j == RING - 1)
                        if tok == NT - 1:
                            last.then_inc(panel_used, 1)
                        elif j == RING - 1:
                            last.then_inc(y_done, 1)
                        if chain is not None and tok >= 2 and j == 1:
                            transposes(chain + tok - 2)

            def down(base, chain):
                for d in range(2):
                    down_panel(base, d, start=d == 0)
                with pe.Fori(0, (NF - 2) // RING - 1) as i:
                    for j in range(RING):
                        down_panel(base, 2 + j, i)
                d0 = NF - RING
                last_rows(base + d0, lambda j: (hs_hi[:, (d0 + j) % RING, :], hs_lo[:, (d0 + j) % RING, :]), chain,
                          (0 if base == DOWN1 else NF) + d0)

            pe.wait_ge(ident_ready, 1)
            for _ in range(WARM_UP):
                nc.tensor.transpose(ps[:, 7, 0:P], ident[:, :], ident[:, :])
            for t in range(2):
                transposes(t)
            up(UP1, 0)
            down(DOWN1, 4)

            def values_to_tokens():
                for tok in range(NT):
                    last = nc.tensor.transpose(ps[:, 1, tok * P:(tok + 1) * P], vT[:, tok * P:(tok + 1) * P], ident[:, :])
                last.then_inc(turned_values, 1)

            def project(i, k, following):
                j = k // 4
                if k == 9:
                    pe.wait_ge(vT_ready, i + 2)
                    values_to_tokens()
                if j >= (4 if following else 2):
                    return
                if k == 0:
                    wait_split(pe, IN + 4, i)
                if k == 4:
                    pe.wait_ge(qm_ready, i + 1)
                    wait_split(pe, IN + 5, i)
                if k == 8:
                    pe.wait_ge(km_ready, i + 1)
                    wait_split(pe, IN + 6, i)
                if k == 12:
                    pe.wait_ge(vm_ready, i + 1)
                    wait_split(pe, IN + 7, i)
                last = columns_product(IN + 4 + j, j % 2, [2 * (k % 4), 2 * (k % 4) + 1])
                if k % 4 == 3:
                    last.then_inc(panel_used, 1)

            def scores(i, k):
                win, e, qt, kts = unit(k)
                g = UNITS * i + k
                if k == 0:
                    if isinstance(i, int) and i == 0:
                        pe.wait_ge(ks_ready, 1)
                    pe.wait_ge(qs_ready, i + 1)
                if k == 1 and isinstance(i, int) and i == 0:
                    pe.wait_ge(qm_ready, 1)
                if k == 8:
                    pe.wait_ge(qm_ready, i + 1)
                    pe.wait_ge(km_ready, i + 1)
                if k >= 2 or not isinstance(i, int) or i > 0:
                    pe.wait_ge(logits_done, g - 1)
                q, k_hi, k_lo = (qs, ks_hi, ks_lo) if win else (qm, km_hi, km_lo)
                queries, keys = slice(qt * P, (qt + 1) * P), slice(kts[0] * P, (kts[-1] + 1) * P)
                dst = ps[:, 2 + k % 2, 0:len(kts) * P]
                nc.tensor.matmul(dst, q[:, e, queries], k_hi[:, e, keys], start=True, stop=False)
                nc.tensor.matmul(dst, q[HALVES[e], e, queries], k_lo[HALVES[e], keys],
                                 start=False, stop=True).then_inc(scores_done, 1)

            def turn(i, k, first):
                win, e, qt, kts = unit(k)
                g = UNITS * i + k
                pe.wait_ge(exp_done, g + 1)
                if k >= 2 or not first:
                    pe.wait_ge(pT_by_act if k % 2 == 0 else pT_by_dve, 8 * i + k // 2)
                for n in range(len(kts)):
                    last = nc.tensor.transpose(ps[:, 4 + k % 2, n * P:(n + 1) * P], prob[:, k % RING, n * P:(n + 1) * P],
                                               ident[:, :])
                last.then_inc(pT_in_psum, 1)

            def values(i, k, first):
                win, e, qt, kts = unit(k)
                pe.wait_ge(pT_by_act if k % 2 == 0 else pT_by_dve, 8 * i + k // 2 + 1)
                if qt == 0 and (k >= 8 or not first):
                    pe.wait_ge(att_done, 4 * i + k // 4 - 1)
                if k == 0 and first:
                    pe.wait_ge(vs_ready, 1)
                if k == 8:
                    pe.wait_ge(vm_ready, i + 1)
                v = vs if win else vm
                for n, kt in enumerate(kts):
                    last = nc.tensor.matmul(ps[:, 6 + k // 4 % 2, qt * HD:(qt + 1) * HD], pT[:, k % 2, n * P:(n + 1) * P],
                                            v[:, kt, HD * e:HD * e + HD], start=n == 0, stop=n == len(kts) - 1)
                last.then_inc(pv_done, 1)

            first_panels(IN, (0, 1, 2, 3), 4)
            pe.wait_ge(vT_ready, 1)
            values_to_tokens()
            pe.wait_ge(ks_ready, 1)

            def att_transposes(h):
                pe.wait_ge(an_ready, h + 1)
                if h == 0:
                    pe.wait_ge(vm_ready, PAIRS)
                elif h < NT:
                    pe.wait_ge(aT_lo_ready, h)
                elif h < NT + 2:
                    pe.wait_ge(att_done, 4 * PAIRS)
                else:
                    pe.wait_ge(aT_lo_ready, h - 1)
                for n in range(4):
                    last = nc.tensor.transpose(ps[:, att_bank(h), n * P:(n + 1) * P],
                                               xn[:, h % 4 // 2, (h % 2 * 4 + n) * P:(h % 2 * 4 + n + 1) * P], ident[:, :])
                last.then_inc(aT_in_psum, 1)

            def window_rows(d, tok, halves=(0, 1)):
                k = W_MOBA // P + d
                return row_products(OUT + d, xT_hi[:, k, :], xT_lo[:, k, :], tok, d == 0, False, halves)

            def window_output(k):
                if 15 <= k < 15 + RING:
                    d = k - 15
                    if k == 15:
                        pe.wait_ge(km_ready, PAIRS)
                        pe.wait_ge(aT_hi_ready, 1)
                        pe.wait_ge(aT_lo_ready, 1)
                    wait_split(pe, OUT + d)
                    window_rows(d, 0, (0,))
                if k in AT_TURN:
                    att_transposes(AT_TURN.index(k))

            def attention(i, first, following):
                for k in range(UNITS if following else UNITS + DRAIN):
                    if k < UNITS:
                        scores(i, k)
                    if has_lagging(k, 2, first):
                        turn(*lagging(i, k, 2), first)
                    if k < UNITS:
                        project(i, k, following)
                    if has_lagging(k, 3, first):
                        values(*lagging(i, k, 3), first)
                    if not following:
                        window_output(k)

            attention(0, True, True)
            with pe.Fori(1, PAIRS - 1) as i:
                attention(i, False, True)
            attention(PAIRS - 1, False, False)

            for d in range(RING):
                for tok in (1, 2):
                    if d == 0:
                        pe.wait_ge(aT_lo_ready, tok + 1)
                    if d == 0 and tok == 1:
                        pe.wait_ge(logits_done, PAIRS * UNITS)
                    elif d == 0:
                        pe.wait_ge(pT_by_act, PAIRS * UNITS // 2)
                        pe.wait_ge(pT_by_dve, PAIRS * UNITS // 2)
                    window_rows(d, tok)
                if d == 0:
                    pe.wait_ge(aT_lo_ready, NT)
                    for row in range(RING):
                        window_rows(row, 0, (1,))
                if d in (0, 2):
                    att_transposes(NT + d)
                    att_transposes(NT + d + 1)
            for d in range(RING):
                if d == 0:
                    pe.wait_ge(aT_lo_ready, 2 * NT)
                window_rows(d, 3).then_inc(panel_used, 1)
            last_rows(OUT + RING, lambda j: (xT_hi[:, j, :], xT_lo[:, j, :]), 8)
            up(UP2, 8)
            down(DOWN2, None)

        @block.scalar
        def _(act):
            def split_hi(c, i=0, first=False):
                wait_loaded(act, c, i)
                if not first:
                    act.wait_ge(panel_used, c + 4 * i - RING + 1)
                nc.scalar.activation(w_hi[:, c % RING, :], raw[:, c % RING, :], ACT.Copy).then_inc(hi_ready, 1)

            squares = []

            def square_sum(src, dst, done, count):
                if len(squares) >= 2:
                    act.wait_ge(*squares[-2])
                nc.scalar.activation(junk[:, len(squares) % 2, 0:src.shape[1]], src, ACT.Square, accum_out=dst) \
                    .then_inc(done, 1)
                squares.append((done, count))

            def sum_y(m):
                if m % NT < NT - 1:
                    act.wait_ge(y_done, (NT - 1) * (m // NT) + m % NT + 1)
                else:
                    act.wait_ge(panel_used, (DOWN1 + NF, OUT + D // P, DOWN2 + NF)[m // NT])
                square_sum(bank2(m % NT), ssy[:, m:m + 1], ssy_done, m + 1)

            def sum_x(n, y=None):
                if y is not None:
                    act.wait_ge(x_ready, y + 1)
                square_sum(xres[:, n % NT, :], ssx[:, n:n + 1], ssx_done, n + 1)

            def turned_hi(n):
                tok = n % NT
                act.wait_ge(xT_in_psum, n + 1)
                for b in range(2):
                    nc.scalar.activation(xT_hi[:, 4 * b:4 * b + 4, tok * P:(tok + 1) * P],
                                         ps[:, 2 * tok + b, :].rearrange("p (k t) -> p k t", t=P), ACT.Copy) \
                        .then_inc(xT_hi_ready, 1)

            def silu(base, i, t):
                n = (0 if base == UP1 else NF) + 2 * i + t
                act.wait_ge(panel_used, base + 4 * i + 2 * t + 1)
                if not isinstance(i, int) or base == UP2:
                    act.wait_ge(h_done, n - 1)
                nc.scalar.activation(tmp[:, 512 * t:512 * t + 512], ps[:, t, :], ACT.Silu).then_inc(silu_done, 1)

            def up(base, down_base):
                for t in range(2):
                    split_hi(base + RING + t)
                    silu(base, 0, t)
                for d in range(2):
                    stage_hidden(down_base, d)
                with act.Fori(1, NF // 2) as i:
                    for t in range(2):
                        for side in range(2):
                            split_hi(base + 2 * t + side + LEAD, i)
                        silu(base, i, t)

            def stage_hidden(base, d, i=0):
                if d >= RING or not isinstance(i, int):
                    act.wait_ge(panel_used, base + d + 4 * i - RING + 1)
                act.wait_ge(h_done, (0 if base == DOWN1 else NF) + d + 4 * i + 1)
                nc.scalar.activation(hs_hi[:, d % RING, :], hT[:, bass.ds(d + 4 * i, 1), :].rearrange("p a t -> p (a t)"),
                                     ACT.Copy).then_inc(hs_hi_ready, 1)

            def down(base, chain):
                for d in range(2):
                    split_hi(base + d + LEAD)
                    stage_hidden(base, d + LEAD)
                with act.Fori(0, (NF - 2) // RING - 1) as i:
                    for j in range(RING):
                        split_hi(base + 2 + j + LEAD, i)
                        stage_hidden(base, 2 + j + LEAD, i)
                for d in range(NF - RING, NF - LEAD):
                    split_hi(base + d + LEAD)
                    stage_hidden(base, d + LEAD)

            def norms(m, n, following):
                sum_y(m)
                sum_x(n, m)
                sum_y(m + 1)
                turned_hi(n)
                sum_x(n + 1, m + 1)
                sum_y(m + 2)
                split_hi(following)
                turned_hi(n + 1)
                sum_x(n + 2, m + 2)
                split_hi(following + 1)
                sum_y(m + 3)
                split_hi(following + 2)
                turned_hi(n + 2)
                sum_x(n + 3, m + 3)
                split_hi(following + 3)
                turned_hi(n + 3)

            for t in range(0, NT, 2):
                for u in (t, t + 1):
                    act.wait_ge(x_loaded[u], 16)
                    sum_x(u)
                split_hi(t, first=True)
                if t == 0:
                    turned_hi(0)
                    turned_hi(1)
                split_hi(t + 1, first=True)
                if t == 2:
                    turned_hi(2)
                    turned_hi(3)
            up(UP1, DOWN1)
            down(DOWN1, 4)
            norms(0, 4, IN)

            def evacuate(dst, wait, count, ready, bank, scale=1.0):
                act.wait_ge(wait, count)
                nc.scalar.activation(dst, ps[:, bank, :], ACT.Copy, scale=scale).then_inc(ready, 1)

            def head_hi(dst, count, ready, bank, scale=1.0, both=False):
                act.wait_ge(panel_used, count)
                for e in range(2):
                    for half in ((e, 1 - e) if both else (e,)):
                        last = nc.scalar.activation(dst[HALVES[half], e, :], ps[HALVES[e], bank, :], ACT.Copy, scale=scale)
                last.then_inc(ready, 1)

            def project(i, k, first, following):
                at = SPLIT_AT if following else LAST_SPLIT_AT
                if k in at:
                    split_hi(IN + 4 + LEAD + at.index(k), i)
                if k == 0 and not first:
                    head_hi(qm, IN + 4 * i + 4, qm_hi_ready, 1, SCALE)
                if k == 4:
                    head_hi(km_hi, IN + 4 * i + 5, km_hi_ready, 0, both=True)
                if k == 10:
                    evacuate(vm[:, :, :].rearrange("p t c -> p (t c)"), turned_values, i + 2, vm_ready, 1)
                if k == 12 and following:
                    head_hi(qs, IN + 4 * i + 7, qs_hi_ready, 0, SCALE)

            def exponent(i, k, first):
                win, e, qt, kts = unit(k)
                g = UNITS * i + k
                act.wait_ge(logits_done, g + 1)
                if k >= RING or not first:
                    act.wait_ge(pT_in_psum, g - RING + 1)
                if k % 4 == 0 and not first:
                    act.wait_ge(att_done, 4 * i + k // 4 - 3)
                if k == 0:
                    act.wait_ge(sink_ready, 3 * (i + 1))
                n = len(kts) * P
                src = s_win[:, e, k % 2, 2 * P - n:2 * P + 1] if win else s_moba[:, k % 2, 0:n]
                nc.scalar.activation(prob[:, k % RING, 0:n + win], src, ACT.Exp, scale=-1.0, bias=nmax[:, k:k + 1],
                                     accum_out=psumrow[:, k:k + 1]).then_inc(exp_done, 1)

            def evacuate_turned(i, k, first):
                if k % 2:
                    return
                n = len(unit(k)[3]) * P
                act.wait_ge(pT_in_psum, UNITS * i + k + 1)
                if k >= 2 or not first:
                    act.wait_ge(pv_done, UNITS * i + k - 1)
                nc.scalar.activation(pT[:, 0, 0:n], ps[:, 4, 0:n], ACT.Copy).then_inc(pT_by_act, 1)

            head_hi(ks_hi, IN + 1, ks_hi_ready, 0, both=True)
            split_hi(IN + 4)
            head_hi(qs, IN + 3, qs_hi_ready, 2, SCALE)
            head_hi(qm, IN + 4, qm_hi_ready, 3, SCALE)
            split_hi(IN + 5)
            evacuate(vs[:, :, :].rearrange("p t c -> p (t c)"), turned_values, 1, vs_ready, 1)

            def sum_att(h):
                square_sum(att[:, h % NT, att_cols(h)], ssa[:, h:h + 1], ssa_done, h + 1)

            def att_hi(h):
                tok, k0 = h % NT, att_cols(h).start // P
                act.wait_ge(aT_in_psum, h + 1)
                nc.scalar.activation(xT_hi[:, k0:k0 + 4, tok * P:(tok + 1) * P],
                                     ps[:, att_bank(h), :].rearrange("p (k t) -> p k t", t=P), ACT.Copy) \
                    .then_inc(aT_hi_ready, 1)

            def window_output(k):
                if k in AT_SQUARE:
                    if k == AT_SQUARE[0]:
                        act.wait_ge(att_done, 4 * PAIRS - 2)
                    sum_att(AT_SQUARE.index(k))
                if k in AT_SPLIT:
                    att_hi(AT_SPLIT.index(k))

            def attention(i, first, following):
                for k in range(UNITS if following else UNITS + DRAIN):
                    if has_lagging(k, 2, first):
                        evacuate_turned(*lagging(i, k, 2), first)
                    if k < UNITS:
                        exponent(i, k, first)
                    if not following:
                        window_output(k)
                    if k < UNITS:
                        project(i, k, first, following)

            attention(0, True, True)
            with act.Fori(1, PAIRS - 1) as i:
                attention(i, False, True)
            attention(PAIRS - 1, False, False)

            att_hi(NT - 1)
            act.wait_ge(att_done, 4 * PAIRS)
            for t in range(NT):
                sum_att(NT + t)
            for t in range(NT):
                att_hi(NT + t)
            for d in range(RING):
                split_hi(OUT + RING + d)
            norms(4, 8, UP2)
            up(UP2, DOWN2)
            down(DOWN2, None)
            for t in range(NT):
                sum_y(8 + t)

        @block.vector
        def _(dve):
            def split_lo(c, i=0):
                dve.wait_ge(hi_ready, c + 4 * i + 1)
                nc.vector.tensor_tensor(w_lo[:, c % RING, :], raw[:, c % RING, :], w_hi[:, c % RING, :].bitcast(F32),
                                        ALU.subtract).then_inc(lo_ready, 1)

            def branch(m, g):
                dve.wait_ge(ssy_done, m + 1)
                if m % NT:
                    dve.wait_ge(x_ready, m)
                nc.vector.tensor_tensor(tmp[:, :], bank2(m % NT), g[:, :], ALU.mult).then_inc(branch_done, 1)

            def residual(m, cols=slice(0, D)):
                dve.wait_ge(branch_done, m + 1)
                dve.wait_ge(rsy_done, m + 1)
                nc.vector.scalar_tensor_tensor(out=xres[:, m % NT, cols], in0=tmp[:, cols], scalar=rsy[:, m:m + 1],
                                               in1=xres[:, m % NT, cols], op0=ALU.mult, op1=ALU.add).then_inc(x_ready, 1)

            def normalise(n, g):
                dve.wait_ge(rsx_done, n + 1)
                if n >= 2:
                    dve.wait_ge(xT_in_psum, n - 1)
                nc.vector.scalar_tensor_tensor(out=xn[:, n % 2, :], in0=xres[:, n % NT, :], scalar=rsx[:, n:n + 1],
                                               in1=g[:, :], op0=ALU.mult, op1=ALU.mult).then_inc(xn_ready, 1)

            def turned_lo(n):
                tok = n % NT
                for b in range(2):
                    dve.wait_ge(xT_hi_ready, 2 * n + b + 1)
                    span = (slice(None), slice(4 * b, 4 * b + 4), slice(tok * P, (tok + 1) * P))
                    nc.vector.tensor_tensor(xT_lo[span], ps[:, 2 * tok + b, :].rearrange("p (k t) -> p k t", t=P),
                                            xT_hi[span].bitcast(F32), ALU.subtract).then_inc(xT_lo_ready, 1)

            def hidden(base, i, t):
                n = (0 if base == UP1 else NF) + 2 * i + t
                dve.wait_ge(silu_done, n + 1)
                dve.wait_ge(panel_used, base + 4 * i + 2 * t + 2)
                nc.vector.tensor_tensor(hT[:, bass.ds(2 * i + t, 1), :].rearrange("p a t -> p (a t)"),
                                        ps[:, 2 + t, :], tmp[:, 512 * t:512 * t + 512], ALU.mult).then_inc(h_done, 1)

            def up(base, down_base):
                for t in range(2):
                    split_lo(base + RING + t)
                    hidden(base, 0, t)
                for d in range(2):
                    stage_hidden(down_base, d)
                with dve.Fori(1, NF // 2) as i:
                    for t in range(2):
                        for side in range(2):
                            split_lo(base + 2 * t + side + LEAD, i)
                        hidden(base, i, t)

            def stage_hidden(base, d, i=0):
                dve.wait_ge(hs_hi_ready, (0 if base == DOWN1 else NF) + d + 4 * i + 1)
                nc.vector.tensor_tensor(hs_lo[:, d % RING, :], hT[:, bass.ds(d + 4 * i, 1), :].rearrange("p a t -> p (a t)"),
                                        hs_hi[:, d % RING, :].bitcast(F32), ALU.subtract).then_inc(hs_lo_ready, 1)

            def down(base):
                for d in range(2):
                    split_lo(base + d + LEAD)
                    stage_hidden(base, d + LEAD)
                with dve.Fori(0, (NF - 2) // RING - 1) as i:
                    for j in range(RING):
                        split_lo(base + 2 + j + LEAD, i)
                        stage_hidden(base, 2 + j + LEAD, i)
                for d in range(NF - RING, NF - LEAD):
                    split_lo(base + d + LEAD)
                    stage_hidden(base, d + LEAD)

            def norms(m, n, g_post, g_pre, following):
                branch(m, g_post)
                residual(m)
                normalise(n, g_pre)
                branch(m + 1, g_post)
                residual(m + 1)
                turned_lo(n)
                normalise(n + 1, g_pre)
                branch(m + 2, g_post)
                residual(m + 2)
                split_lo(following)
                turned_lo(n + 1)
                split_lo(following + 1)
                normalise(n + 2, g_pre)
                branch(m + 3, g_post)
                residual(m + 3)
                split_lo(following + 2)
                turned_lo(n + 2)
                normalise(n + 3, g_pre)
                split_lo(following + 3)
                turned_lo(n + 3)

            dve.wait_ge(gain_a, 16)
            for t in range(0, NT, 2):
                normalise(t, g_a)
                normalise(t + 1, g_a)
                split_lo(t)
                if t == 0:
                    turned_lo(0)
                    turned_lo(1)
                split_lo(t + 1)
                if t == 2:
                    turned_lo(2)
                    turned_lo(3)
            up(UP1, DOWN1)
            down(DOWN1)
            dve.wait_ge(gain_b, 16)
            dve.wait_ge(gain_c, 16)
            norms(0, 4, g_b, g_c, IN)

            def evacuate(dst, count, ready, bank):
                dve.wait_ge(panel_used, count)
                nc.vector.tensor_copy(dst, ps[:, bank, :]).then_inc(ready, 1)

            def queries_lo(q, hi_ready_, count, ready, bank):
                dve.wait_ge(hi_ready_, count)
                for e in range(2):
                    last = nc.vector.scalar_tensor_tensor(out=q[HALVES[1 - e], e, :], in0=ps[HALVES[e], bank, :],
                                                          scalar=SCALE, in1=q[HALVES[e], e, :].bitcast(F32),
                                                          op0=ALU.mult, op1=ALU.subtract)
                last.then_inc(ready, 1)

            def keys_lo(k_hi, k_lo, hi_ready_, count, ready):
                dve.wait_ge(hi_ready_, count)
                for e in range(2):
                    last = nc.vector.tensor_tensor(k_lo[HALVES[e], :], ps[HALVES[e], 0, :],
                                                   k_hi[HALVES[e], e, :].bitcast(F32), ALU.subtract)
                last.then_inc(ready, 1)

            def project(i, k, first, following):
                at = SPLIT_AT if following else LAST_SPLIT_AT
                if k in at:
                    split_lo(IN + 4 + LEAD + at.index(k), i)
                if k == 1 and not first:
                    queries_lo(qm, qm_hi_ready, i + 1, qm_ready, 1)
                if k == 6:
                    keys_lo(km_hi, km_lo, km_hi_ready, i + 1, km_ready)
                if k == 8:
                    evacuate(vT[:, :], IN + 4 * i + 6, vT_ready, 1)
                if k == 14 and following:
                    queries_lo(qs, qs_hi_ready, i + 2, qs_ready, 0)

            def logits(i, k, first):
                win, e, qt, kts = unit(k)
                g = UNITS * i + k
                dve.wait_ge(scores_done, g + 1)
                if k >= 2 or not first:
                    dve.wait_ge(exp_done, g - 1)
                n = len(kts) * P
                if k == 0:
                    dve.wait_ge(bias_s_loaded, 16 * (i + 1))
                    dve.wait_ge(sink_ready, 3 * (i + 1))
                if k == 8:
                    dve.wait_ge(bias_m_loaded, 16 * (i + 1))
                if not isinstance(i, int):
                    hold_here(dve, dve_held)
                nc.vector.tensor_tensor_reduce(
                    out=s_win[:, e, k % 2, 2 * P - n:2 * P] if win else s_moba[:, k % 2, 0:n],
                    in0=ps[:, 2 + k % 2, 0:n], in1=bias_s[:, e, 2 * P - n:2 * P] if win else bias_m[:, e, T - n:T],
                    scale=-1.0, scalar=nsink_now[:, e:e + 1] if win else BIG, op0=ALU.add, op1=ALU.min,
                    accum_out=nmax[:, k:k + 1]).then_inc(logits_done, 1)

            def evacuate_turned(i, k, first):
                if k % 2 == 0:
                    return
                n = len(unit(k)[3]) * P
                dve.wait_ge(pT_in_psum, UNITS * i + k + 1)
                if k >= 2 or not first:
                    dve.wait_ge(pv_done, UNITS * i + k - 1)
                nc.vector.tensor_copy(pT[:, 1, 0:n], ps[:, 5, 0:n]).then_inc(pT_by_dve, 1)

            def head_done(i, h):
                g = 4 * i + h
                win, e = h < 2, h % 2
                dve.wait_ge(pv_done, 4 * (g + 1))
                dve.wait_ge(exp_done, 4 * (g + 1))
                nc.vector.reciprocal(rinv[:, 4 * h:4 * h + 4], psumrow[:, 4 * h:4 * h + 4]).then_inc(rinv_done, 1)
                dve.wait_ge(rinv_done, g + 1)
                col = W_MOBA + (i + 4 * e) * HD if win else (2 * i + e) * HD
                nc.vector.tensor_tensor(att[:, :, bass.ds(col, HD)],
                                        ps[:, 6 + e, 0:4 * HD].rearrange("p (t c) -> p t c", c=HD),
                                        rinv[:, 4 * h:4 * h + 4].rearrange("p (t a) -> p t a", a=1)
                                        .to_broadcast([P, NT, HD]), ALU.mult).then_inc(att_done, 1)

            evacuate(vT[:, :], IN + 2, vT_ready, 1)
            keys_lo(ks_hi, ks_lo, ks_hi_ready, 1, ks_ready)
            split_lo(IN + 4)
            queries_lo(qs, qs_hi_ready, 1, qs_ready, 2)
            queries_lo(qm, qm_hi_ready, 1, qm_ready, 3)
            split_lo(IN + 5)

            def normalise_att(h):
                dve.wait_ge(rsa_done, h + 1)
                if h >= NT:
                    dve.wait_ge(aT_in_psum, h - NT + 1)
                cols = att_cols(h)
                nc.vector.scalar_tensor_tensor(out=xn[:, h % 4 // 2, h % 2 * 512:(h % 2 + 1) * 512],
                                               in0=att[:, h % NT, cols], scalar=rsa[:, h:h + 1], in1=g_a[:, cols],
                                               op0=ALU.mult, op1=ALU.mult).then_inc(an_ready, 1)

            def att_lo(h):
                tok, k0 = h % NT, att_cols(h).start // P
                dve.wait_ge(aT_hi_ready, h + 1)
                span = (slice(None), slice(k0, k0 + 4), slice(tok * P, (tok + 1) * P))
                nc.vector.tensor_tensor(xT_lo[span], ps[:, att_bank(h), :].rearrange("p (k t) -> p k t", t=P),
                                        xT_hi[span].bitcast(F32), ALU.subtract).then_inc(aT_lo_ready, 1)

            def window_output(k):
                if k in AT_NORMALISE:
                    if k == AT_NORMALISE[0]:
                        dve.wait_ge(gain_a, 48)
                    normalise_att(AT_NORMALISE.index(k))
                if k in AT_SPLIT:
                    att_lo(AT_SPLIT.index(k))

            def attention(i, first, following):
                for k in range(UNITS if following else UNITS + DRAIN):
                    if k < UNITS:
                        logits(i, k, first)
                    if has_lagging(k, 2, first):
                        evacuate_turned(*lagging(i, k, 2), first)
                    if k in (7, 10, 15):
                        head_done(i, (k - 6) // 4)
                    if k == 3 and not first:
                        head_done(i - 1, 3)
                    if not following:
                        window_output(k)
                    if k < UNITS:
                        project(i, k, first, following)
                if not following:
                    head_done(i, 3)

            attention(0, True, True)
            with dve.Fori(1, PAIRS - 1) as i:
                attention(i, False, True)
            attention(PAIRS - 1, False, False)

            att_lo(NT - 1)
            for t in range(NT):
                normalise_att(NT + t)
                if t >= 1:
                    att_lo(NT + t - 1)
            att_lo(2 * NT - 1)
            for d in range(RING):
                split_lo(OUT + RING + d)
            dve.wait_ge(gain_b, 32)
            dve.wait_ge(gain_c, 32)
            norms(4, 8, g_b, g_c, UP2)
            up(UP2, DOWN2)
            down(DOWN2)
            dve.wait_ge(gain_d, 16)
            for t in range(NT - 1):
                branch(8 + t, g_d)
                residual(8 + t)
            branch(8 + NT - 1, g_d)
            for half in range(2):
                residual(8 + NT - 1, slice(D // 2 * half, D // 2 * (half + 1)))


_INS = ['x', 'ffn1_pre_g', 'ffn1_w_gate', 'ffn1_w_up', 'ffn1_w_down', 'ffn1_post_g', 'mix_pre_g', 'w_in', 'rel_bias',
        'moba_out_g', 'swa_sinks', 'swa_out_g', 'w_out', 'mix_post_g', 'ffn2_pre_g', 'ffn2_w_gate', 'ffn2_w_up',
        'ffn2_w_down', 'ffn2_post_g']
_OUTS = [((1, T, D), 'float32')]


def kernel(**inputs):
    import numpy as _np
    import concourse.bacc as _bacc
    from concourse import mybir as _mybir
    from concourse.bass_utils import run_bass_kernel_spmd as _run

    nc = _bacc.Bacc("TRN2", target_bir_lowering=False, num_devices=1)
    arrays, args = {}, []
    for name in _INS:
        a = _np.ascontiguousarray(inputs[name])
        arrays[f"in_{name}_dram"] = a
        args.append(nc.dram_tensor(f"in_{name}_dram", a.shape, _mybir.dt.from_np(a.dtype), kind="ExternalInput").ap())
    for i, (shape, dtype) in enumerate(_OUTS):
        dt = _mybir.dt.from_np(_np.dtype(dtype))
        args.append(nc.dram_tensor(f"out_{i}_dram", shape, dt, kind="ExternalOutput").ap())
    build(nc, *args)
    r = _run(nc, [arrays], core_ids=[0])
    got = tuple(r.results[0][f"out_{i}_dram"] for i in range(len(_OUTS)))
    return got[0]
```
